# Optimizing a Trainium2 kernel written in Bass

```python
import math
import jax, jax.numpy as jnp
from jax import lax
import numpy as np

D_MODEL = 1024
BATCH = 1
SEQ = 1024
DEPTH = 2

N_MIXERS = 2
N_CONV = (DEPTH + 1) // 2
N_ATTN = DEPTH // 2
CONV_WIDTH = 3
HEAD_DIM = 64
N_HEADS = D_MODEL // HEAD_DIM
Q_BLOCK = 128
RMS_EPS = 1e-6

kernel_name = "hybrid_shortconv_forgetting_attention"

def _rmsnorm(x, g):
    xf = x.astype(jnp.float32)
    inv = lax.rsqrt(jnp.mean(xf * xf, axis=-1, keepdims=True) + RMS_EPS)
    return (xf * inv * g.astype(jnp.float32)).astype(x.dtype)

def _short_conv_layer(x, norm_g, w_in, conv_w, w_out):
    h = _rmsnorm(x, norm_g)
    proj = jnp.einsum('bsd,de->bse', h, w_in)
    b_g, c_g, xin, z = jnp.split(proj, 4, axis=-1)
    u = c_g * xin
    y = lax.conv_general_dilated(
        u, conv_w[:, None, :].astype(u.dtype),
        window_strides=(1,), padding=[(CONV_WIDTH - 1, 0)],
        dimension_numbers=('NWC', 'WIO', 'NWC'),
        feature_group_count=D_MODEL)
    y = b_g * y * jax.nn.silu(z)
    return x + jnp.einsum('bse,ed->bsd', y, w_out)

def _forgetting_attention(q, k, v, log_f):
    S = q.shape[2]
    c = jnp.cumsum(log_f, axis=-1)
    scale = 1.0 / math.sqrt(HEAD_DIM)
    kpos = jnp.arange(S)
    neg = jnp.finfo(jnp.float32).min

    def block(i):
        start = i * Q_BLOCK
        qb = lax.dynamic_slice_in_dim(q, start, Q_BLOCK, axis=2)
        cb = lax.dynamic_slice_in_dim(c, start, Q_BLOCK, axis=2)
        s = jnp.einsum('bhqd,bhkd->bhqk', qb, k) * scale
        s = s + cb[..., :, None] - c[..., None, :]
        qpos = start + jnp.arange(Q_BLOCK)
        s = jnp.where(kpos[None, :] <= qpos[:, None], s, neg)
        p = jax.nn.softmax(s, axis=-1)
        return jnp.einsum('bhqk,bhkd->bhqd', p, v)

    out = lax.map(block, jnp.arange(S // Q_BLOCK))
    nb, b, h, qn, dh = out.shape
    return jnp.transpose(out, (1, 2, 0, 3, 4)).reshape(b, h, nb * qn, dh)

def _attn_layer(x, norm_g, w_in, b_f, q_g, k_g, w_out):
    B, S, D = x.shape
    h = _rmsnorm(x, norm_g)
    proj = jnp.einsum('bsd,de->bse', h, w_in)
    q = proj[..., 0 * D:1 * D]
    k = proj[..., 1 * D:2 * D]
    v = proj[..., 2 * D:3 * D]
    z = proj[..., 3 * D:4 * D]
    f_logit = proj[..., 4 * D:].astype(jnp.float32) + b_f.astype(jnp.float32)
    to_heads = lambda t: jnp.transpose(t.reshape(B, S, N_HEADS, HEAD_DIM), (0, 2, 1, 3))
    q = _rmsnorm(to_heads(q), q_g).astype(jnp.float32)
    k = _rmsnorm(to_heads(k), k_g).astype(jnp.float32)
    v = to_heads(v).astype(jnp.float32)
    log_f = jnp.transpose(jax.nn.log_sigmoid(f_logit), (0, 2, 1))
    o = _forgetting_attention(q, k, v, log_f)
    o = jnp.transpose(o, (0, 2, 1, 3)).reshape(B, S, D).astype(x.dtype)
    o = o * jax.nn.silu(z)
    return x + jnp.einsum('bse,ed->bsd', o, w_out)

def setup_inputs(seed: int = 0) -> dict:
    key = jax.random.key(seed)
    ks = jax.random.split(key, 12)
    D = D_MODEL
    s_d = D ** -0.5
    x = jax.random.normal(ks[0], (BATCH, SEQ, D), jnp.float32)
    conv_norm_g = 1.0 + 0.02 * jax.random.normal(ks[1], (N_CONV, D), jnp.float32)
    conv_w_in = jax.random.normal(ks[2], (N_CONV, D, 4 * D), jnp.float32) * s_d
    conv_w = jax.random.normal(ks[3], (N_CONV, CONV_WIDTH, D), jnp.float32) * (CONV_WIDTH ** -0.5)
    conv_w_out = jax.random.normal(ks[4], (N_CONV, D, D), jnp.float32) * s_d
    attn_norm_g = 1.0 + 0.02 * jax.random.normal(ks[5], (N_ATTN, D), jnp.float32)
    attn_w_in = jax.random.normal(ks[6], (N_ATTN, D, 4 * D + N_HEADS), jnp.float32) * s_d
    attn_b_f = jax.random.uniform(ks[7], (N_ATTN, N_HEADS), jnp.float32, 1.0, 4.0)
    attn_q_norm_g = 1.0 + 0.02 * jax.random.normal(ks[8], (N_ATTN, HEAD_DIM), jnp.float32)
    attn_k_norm_g = 1.0 + 0.02 * jax.random.normal(ks[9], (N_ATTN, HEAD_DIM), jnp.float32)
    attn_w_out = jax.random.normal(ks[10], (N_ATTN, D, D), jnp.float32) * s_d
    return {"x": x, "conv_norm_g": conv_norm_g, "conv_w_in": conv_w_in, "conv_w": conv_w,
            "conv_w_out": conv_w_out, "attn_norm_g": attn_norm_g, "attn_w_in": attn_w_in,
            "attn_b_f": attn_b_f, "attn_q_norm_g": attn_q_norm_g, "attn_k_norm_g": attn_k_norm_g,
            "attn_w_out": attn_w_out}

def reference(x, conv_norm_g, conv_w_in, conv_w, conv_w_out, attn_norm_g, attn_w_in,
              attn_b_f, attn_q_norm_g, attn_k_norm_g, attn_w_out):
    for i in range(DEPTH):
        j = i // N_MIXERS
        if i % N_MIXERS == 0:
            x = _short_conv_layer(x, conv_norm_g[j], conv_w_in[j], conv_w[j], conv_w_out[j])
        else:
            x = _attn_layer(x, attn_norm_g[j], attn_w_in[j], attn_b_f[j],
                            attn_q_norm_g[j], attn_k_norm_g[j], attn_w_out[j])
    return x


_drawn_inputs = setup_inputs


def setup_inputs(seed=0):
    import zlib

    import numpy as np

    out = dict(_drawn_inputs(seed))
    spreads = {}
    factors = {'attn_norm_g': 7.692, 'attn_q_norm_g': 8.0, 'attn_k_norm_g': 8.0}
    for name, (base, spread) in spreads.items():
        noise = np.random.default_rng([zlib.crc32(name.encode()), seed]).standard_normal(out[name].shape)
        drawn = base * np.exp(spread * noise) if base else spread * noise
        out[name] = __import__('jax').numpy.asarray(drawn.astype(out[name].dtype))
    for name, factor in factors.items():
        out[name] = (out[name] * factor).astype(out[name].dtype)
    return out
```

```python
import concourse.bass as bass
from concourse import mybir
from contextlib import ExitStack

F32 = mybir.dt.float32
F32R = mybir.dt.float32r
BF16 = mybir.dt.bfloat16
ALU = mybir.AluOpType
ACT = mybir.ActivationFunctionType
AX = mybir.AxisListType

P = 128
D = 1024
S = 1024
KT = D // P
NH = 16
DH = D // NH
PAIRS = NH // 2
HALF = S // 2
TAPS = 3
EPS = 1e-6
MASKED = -3.0e38

N_CIN, N_COUT, N_FORGET, N_AIN, N_AOUT = 0, 4 * KT, 5 * KT, 5 * KT + 1, 9 * KT + 1
N_TILES = 10 * KT + 1
CONV_COLUMNS = [1, 2, 3, 0]
B_PROJ, B_SCORE, B_PT, B_OUT, B_MISC = 0, 2, 4, 6, 7
STEPS = [(x, t) for x in range(2) for t in (3, 2, 1, 0)]
CHUNK0 = [0, 4, 7, 9, 10, 14, 17, 19]
CHUNKS = 20


def counted(value):
    return not isinstance(value, int) or value > 0


def hybrid(nc, x, w_cin, w_cout, w_ain, w_forget, w_aout, conv_gain, conv_taps, attn_gain, b_forget,
           q_gain, k_gain, out):
    x1_dram = nc.dram_tensor("x1_dram", [P, KT, S], F32, kind="Internal").ap()
    c_dram = nc.dram_tensor("c_dram", [NH, 4, S], F32, kind="Internal").ap()

    with ExitStack() as ctx:
        def sb(name, shape, dt=F32, where=ctx):
            return where.enter_context(nc.sbuf_tensor(name, shape, dt))

        def sem(name):
            return ctx.enter_context(nc.semaphore(name))

        ps = ctx.enter_context(nc.psum_tensor("ps", [P, 8, HALF], F32))

        h_hi = sb("h_hi", [P, KT, S], F32R)
        h_lo = sb("h_lo", [P, KT, S], F32R)
        w_raw = sb("w_raw", [P, 2, KT, P])
        w_hi = sb("w_hi", [P, 2, KT, P], F32R)
        w_lo = sb("w_lo", [P, 2, KT, P], F32R)
        inv = sb("inv", [P, S])
        scr = sb("scr", [P, 3 * S])
        ubuf = sb("ubuf", [P, S + 8])
        ident = sb("ident", [P, P])
        ident_bf = sb("ident_bf", [P, P], BF16)
        mask_bf = sb("mask_bf", [P, 2 * P], BF16)
        mean_d = sb("mean_d", [P, P])
        mean_h = sb("mean_h", [P, P])
        g1 = sb("g1", [P, KT])
        g2 = sb("g2", [P, KT])
        taps = sb("taps", [P, TAPS, KT])
        gq = sb("gq", [P, 1])
        gk = sb("gk", [P, 1])
        b_f = sb("b_f", [NH, 1])
        eps_col = sb("eps_col", [P, 1])
        neg_max = sb("neg_max", [P, 4])
        denom = sb("denom", [P, 4])
        rdenom = sb("rdenom", [P, 4])

        acc = scr[:, 0:S]
        sq2 = scr[:, S:2 * S]
        mbuf = scr[:, 2 * S:3 * S]
        ca = scr[:, 0:S]
        gate = scr[:, S:2 * S]
        yb = scr[:, 2 * S:3 * S]
        sq = scr[:, 0:HALF]
        y0 = scr[:, HALF:S]
        osum = scr[:, S:S + HALF]
        p_small = scr[:, S + HALF:3 * S].rearrange("p (b n) -> p b n", b=2)
        v_t = ubuf[:, 0:S]

        conv_ctx = ExitStack()
        x_t = sb("x_t", [P, KT, S], where=conv_ctx)
        y_hi = sb("y_hi", [P, KT, S], F32R, where=conv_ctx)
        y_lo = sb("y_lo", [P, KT, S], F32R, where=conv_ctx)
        conv_ctx.close()

        y2 = sb("y2", [P, KT, S])
        q1 = sb("q1", [P, 2, S], F32R)
        k1 = sb("k1", [P, 2, S], F32R)
        q2 = sb("q2", [P, 2, S], F32R)
        k2 = sb("k2", [P, 2, S], F32R)
        qn = sb("qn", [P, S])
        kn = sb("kn", [P, S])
        v_st = sb("v_st", [P, 2, KT, P], F32R)
        p_big = sb("p_big", [P, 2, S])
        pt_hi = sb("pt_hi", [P, 2, HALF], F32R)
        pt_lo = sb("pt_lo", [P, 2, HALF], F32R)

        s_const = sem("const_landed")
        s_ident = sem("identity_made")
        s_vconst = sem("constants_made")
        s_x = [sem(f"x_landed{i}") for i in range(4)]
        s_wraw = [sem(f"w_landed{i}") for i in range(2)]
        s_whi = sem("w_hi_made")
        s_wlo = sem("w_lo_made")
        s_unit = sem("units_done")
        s_sqm = sem("squares_made")
        s_sqa = sem("squares_added")
        s_h = sem("h_ready")
        s_ms = sem("mean_square_done")
        s_msr = sem("mean_square_read")
        s_rs0 = sem("rsqrt_guessed")
        s_inv = sem("inv_ready")
        s_evac = sem("conv_units_evacuated")
        s_u = sem("u_scaled")
        s_gate = sem("gate_made")
        s_y = sem("y_made")
        s_yhi = sem("y_hi_made")
        s_ylo = sem("y_lo_made")
        s_spill = sem("x1_stored")
        s_clear = sem("stacks_cleared")
        s_f = sem("forget_steps")
        s_fa = sem("forget_act_steps")
        s_cst = sem("c_stored")
        s_crow = [sem(f"c_rows_landed{i}") for i in range(2)]
        s_qkraw = sem("qk_evacuated")
        s_vz = sem("vz_evacuated")
        s_qsq = sem("qk_squared")
        s_ssq = sem("head_square_done")
        s_guess = sem("head_rsqrt_guessed")
        s_qkn = sem("qk_normed")
        s_sthi = sem("stack_hi_made")
        s_stq = sem("stack_q_lo_made")
        s_stk = sem("stack_k_lo_made")
        s_vtr = sem("v_transposed")
        s_vhi = sem("v_hi_made")
        s_vlo = sem("v_lo_made")
        s_sc = sem("scores_done")
        s_max = sem("row_max_done")
        s_exp = sem("exp_done")
        s_rd = sem("denominators_inverted")
        s_pn = sem("p_normalised")
        s_ptr = sem("p_transposed")
        s_pth = sem("pt_hi_made")
        s_ptl = sem("pt_lo_made")
        s_pv = sem("pv_done")
        s_oc = sem("out_lo_half_copied")
        s_os = sem("out_halves_summed")
        s_y2 = sem("y2_made")
        s_ze = sem("z_exp_done")
        s_gz = sem("z_gate_made")
        s_y2h = sem("y2_hi_made")
        s_y2l = sem("y2_lo_made")
        s_x1r = [sem(f"x1_reloaded{i}") for i in range(2)]
        s_or = sem("out_residual_added")
        s_out = [sem(f"out_stored{i}") for i in range(4)]
        s_dve = sem("vector_steps")
        s_zero = sem("sums_cleared")

        block = ctx.enter_context(nc.Block())

        def halves(h):
            return slice(h * HALF, (h + 1) * HALF)

        @block.sync
        def _(sp):
            def load_w(src, n, slot, tile):
                if counted(n - 1):
                    sp.wait_ge(s_whi, n - 1)
                    sp.wait_ge(s_wlo, n - 1)
                sp.dma_start(w_raw[:, slot, :, :], src[tile]).then_inc(s_wraw[slot], 16)

            def load_x(i):
                h, ks = i // 2, slice(4 * (i % 2), 4 * (i % 2) + 4)
                sp.dma_start(x_t[:, ks, halves(h)], x[:, ks, halves(h)]).then_inc(s_x[i], 16)

            load_x(0)
            load_w(w_cin, 0, 0, 0)
            load_x(1)
            load_w(w_cin, 1, 1, 1)
            load_x(2)
            load_x(3)
            load_w(w_cin, 2, 0, 2)
            load_w(w_cin, 3, 1, 3)
            with sp.Fori(1, KT) as j:
                for t in range(4):
                    load_w(w_cin, 4 * j + t, t % 2, 4 * j + t)
            for m in range(KT + 3):
                if m < KT:
                    load_w(w_cout, N_COUT + m, m % 2, m)
                elif m == KT:
                    sp.wait_ge(s_whi, N_FORGET - 1)
                    sp.wait_ge(s_wlo, N_FORGET - 1)
                    sp.dma_start(w_raw[:, 0, :, 0:NH], w_forget).then_inc(s_wraw[0], 16)
                else:
                    load_w(w_ain, N_AIN + m - KT - 1, m % 2, m - KT - 1)
                if m >= 3:
                    sp.wait_ge(s_evac, 8 * KT + 2 * (m - 3) + 2)
                    sp.dma_start(x1_dram[:, m - 3, :], x_t[:, m - 3, :]).then_inc(s_spill, 16)
            sp.wait_ge(s_fa, 3)
            sp.dma_start(c_dram[:, 0, :], pt_hi[0:NH, :, :].bitcast(F32)).then_inc(s_cst, 16)
            sp.wait_ge(s_f, 6)
            sp.dma_start(c_dram[:, 1, :], pt_lo[0:NH, :, :].bitcast(F32)).then_inc(s_cst, 16)
            sp.wait_ge(s_fa, 4)
            sp.dma_start(c_dram[:, 2, :], v_st[0:NH, 0, :, :].bitcast(F32)).then_inc(s_cst, 16)
            sp.wait_ge(s_fa, 5)
            sp.dma_start(c_dram[:, 3, :], v_st[0:NH, 1, :, :].bitcast(F32)).then_inc(s_cst, 16)

            def c_rows(side, pair):
                own = P // 2 * (1 - side)
                head = 2 * pair + side
                sp.dma_start(q2[own:own + 2, side, :].bitcast(F32), c_dram[bass.ds(head, 1), 0:2, :]
                             .rearrange("a c s -> (a c) s")).then_inc(s_crow[side], 16)
                sp.dma_start(k2[own + 2:own + 4, side, :].bitcast(F32), c_dram[bass.ds(head, 1), 2:4, :]
                             .rearrange("a c s -> (a c) s")).then_inc(s_crow[side], 16)

            def iteration(it, proj, att):
                pair = it - 1
                if att:
                    if counted(16 * pair):
                        sp.wait_ge(s_sc, 16 * pair)
                    c_rows(1, pair)
                if proj:
                    n = N_AIN + 4 * it
                    for t in range(4):
                        m = n + 2 + t
                        if not isinstance(it, int) or 4 * it + t + 2 < 4 * PAIRS:
                            load_w(w_ain, m, (N_AIN + t) % 2, 4 * it + t + 2)
                        else:
                            load_w(w_aout, m, (N_AIN + t) % 2, t - 2)
                        if t == 2:
                            if counted(16 * pair + 8):
                                sp.wait_ge(s_sc, 16 * pair + 8)
                            if isinstance(it, int) and it == 0:
                                sp.wait_ge(s_cst, 64)
                                sp.wait_ge(s_clear, 1)
                            c_rows(0, it)

            iteration(0, True, False)
            iteration(1, True, True)
            with sp.Fori(2, PAIRS - 1) as it:
                iteration(it, True, True)
            iteration(PAIRS - 1, True, True)
            iteration(PAIRS, False, True)
            def store_out(m):
                for h in range(2):
                    sp.wait_ge(s_or, 2 * m + h + 1)
                    sp.dma_start(out[:, m, halves(h)], p_big[:, m % 2, halves(h)])\
                        .then_inc(s_out[2 * (m % 2) + h], 16)

            sp.wait_ge(s_spill, 16 * KT)
            for m in range(KT):
                if m >= 2:
                    load_w(w_aout, N_AOUT + m, (N_AOUT + m) % 2, m)
                sp.wait_ge(s_stk, 2 * PAIRS)
                sp.wait_ge(s_stq, 2 * PAIRS)
                sp.wait_ge(s_sthi, 2 * PAIRS)
                if counted(2 * (m - 2) + 2):
                    sp.wait_ge(s_or, 2 * (m - 2) + 2)
                sp.dma_start((qn, kn)[m % 2][:, :], x1_dram[:, m, :]).then_inc(s_x1r[m % 2], 16)
                if m >= 2:
                    store_out(m - 2)
            store_out(KT - 2)
            store_out(KT - 1)
            for i in range(4):
                sp.wait_ge(s_out[i], 16 * (KT // 2))

        @block.tensor
        def _(pe):
            mm = nc.tensor.matmul

            def unit_part(slot, bank, h, ks, mov_hi, mov_lo, ready=None, first=0, step=0):
                last = None
                for k in ks:
                    if ready is not None:
                        pe.wait_ge(ready, first + step * k)
                    for st, mov in ((w_hi, mov_hi), (w_hi, mov_lo), (w_lo, mov_hi)):
                        last = mm(ps[:, bank, :], st[:, slot, k, :], mov[:, k, halves(h)],
                                  start=(k == 0 and st is w_hi and mov is mov_hi),
                                  stop=(k == KT - 1 and st is w_lo))
                return last

            def mean_square(turn, banks):
                for h in range(2):
                    pe.wait_ge(s_sqa, turn * 2 * KT + 2 * KT - (1 - h) * (KT if turn == 0 else 1))
                    mm(ps[:, banks + h, :], mean_d[:, :], acc[:, halves(h)], start=True, stop=True)\
                        .then_inc(s_ms, 1)

            pe.wait_ge(s_vconst, 1)
            pe.wait_ge(s_ident, 3)
            mean_square(0, 4)

            def conv_block(j, first):
                for t in range(4):
                    n = 4 * j + t
                    pe.wait_ge(s_wlo, n + 1)
                    for h in range(2):
                        u = 2 * t + h
                        if first:
                            if t == 2:
                                pe.wait_ge(s_msr, h + 1)
                        else:
                            pe.wait_ge(s_evac, 8 * j + u - 7)
                        unit_part(t % 2, u, h, range(KT), h_hi, h_lo,
                                  s_h if first and t == 0 else None, KT * h + 1, 1).then_inc(s_unit, 1)

            conv_block(0, True)
            with pe.Fori(1, KT) as j:
                conv_block(j, False)

            with pe.Fori(0, 2) as i:
                for t in range(4):
                    pe.wait_ge(s_wlo, N_COUT + 4 * i + t + 1)
                    for h in range(2):
                        u = 2 * t + h
                        pe.wait_ge(s_evac, 8 * KT + 8 * i + u - 7)
                        unit_part(t % 2, u, h, range(KT), y_hi, y_lo,
                                  s_ylo if t == 0 else None, h + 1, 2).then_inc(s_unit, 1)

            pe.wait_ge(s_wlo, N_FORGET + 1)
            for h in range(2):
                pe.wait_ge(s_evac, 10 * KT - 8 + h + 1)
                unit_part(0, h, h, range(KT), h_hi, h_lo,
                          s_h, 2 * KT + h + 1, 2).then_inc(s_unit, 1)
            pe.wait_ge(s_evac, 10 * KT)
            mean_square(1, 2)

            def scores(it, i, par):
                pair = it - 1
                side, t = STEPS[i]
                if t == 3 and par == 0:
                    pe.wait_ge(s_sthi, 2 * pair + side + 1)
                    pe.wait_ge(s_stq, 2 * pair + side + 1)
                    pe.wait_ge(s_stk, 2 * pair + side + 1)
                    pe.wait_ge(s_crow[side], 32 * pair + 32)
                if counted(16 * pair + 2 * i + (par if t >= 2 else 0 if t == 1 else par - 1)):
                    pe.wait_ge(s_exp, 16 * pair + 2 * i + (par if t >= 2 else 0 if t == 1 else par - 1))
                qs = (2 * t + par) * P
                n, w = (2, P * (t + 1)) if t >= 2 else (1, 2 * P * (t + 1))
                for c in range(n):
                    bank = B_SCORE + (c if t >= 2 else par)
                    last_c = c == n - 1
                    for a, b in ((q1, k1), (q2, k2)):
                        last = mm(ps[:, bank, 0:w], a[:, side, qs:qs + P], b[:, side, c * w:(c + 1) * w],
                                  start=(a is q1), stop=(a is q2 and not last_c))
                    if last_c:
                        lo = 2 * P * t - c * w + par * P
                        mw = 2 * P - par * P
                        last = mm(ps[:, bank, lo:lo + mw], ident_bf[:, :], mask_bf[:, 0:mw],
                                  start=False, stop=True)
                last.then_inc(s_sc, 1)

            def transpose_p(it, i, c):
                pair = it - 1
                t = STEPS[i][1]
                g = CHUNK0[i] + c
                if c == 0:
                    pe.wait_ge(s_pn, 16 * pair + 2 * i + 2)
                if counted(CHUNKS * pair + g - 1):
                    pe.wait_ge(s_ptl, CHUNKS * pair + g - 1)
                src = p_big if i % 2 == 0 else p_small
                for kp in range(2):
                    for par in range(2):
                        at = (2 * kp + par) * P
                        last = nc.tensor.transpose(ps[:, B_PT + g % 2, at:at + P],
                                                   src[:, par, (2 * c + kp) * P:(2 * c + kp + 1) * P],
                                                   ident[:, :])
                last.then_inc(s_ptr, 1)

            def pv(it, i, c):
                pair = it - 1
                side, t = STEPS[i]
                g = CHUNK0[i] + c
                if c == 0 and t % 2 == 1:
                    if counted(4 * pair + 2 * side + (0 if t == 3 else 1)):
                        pe.wait_ge(s_os, 4 * pair + 2 * side + (0 if t == 3 else 1))
                    pe.wait_ge(s_vlo, 2 * pair + side + 1)
                pe.wait_ge(s_ptl, CHUNKS * pair + g + 1)
                at = (t % 2) * 2 * P
                for kp in range(2):
                    for mov in (pt_hi, pt_lo):
                        last = mm(ps[:, B_OUT, at:at + 2 * P], v_st[:, side, 2 * c + kp, :],
                                  mov[:, g % 2, kp * 2 * P:(kp + 1) * 2 * P],
                                  start=(c == 0 and kp == 0 and mov is pt_hi),
                                  stop=(c == t and kp == 1 and mov is pt_lo))
                last.then_inc(s_pv, 1)

            def head_square(it, u):
                if u == 0:
                    if counted(2 * it):
                        pe.wait_ge(s_vlo, 2 * it)
                if counted(4 * it + u):
                    pe.wait_ge(s_qkn, 4 * it + u)
                pe.wait_ge(s_qsq, 4 * it + u + 1)
                mm(ps[:, B_MISC, :], mean_h[:, :], sq, start=True, stop=True).then_inc(s_ssq, 1)

            def transpose_v(side):
                r = DH * side
                for k in range(KT):
                    last = nc.tensor.transpose(ps[:, B_MISC, k * DH:(k + 1) * DH],
                                               v_t[r:r + DH, k * P:(k + 1) * P],
                                               ident[r:r + DH, r:r + DH])
                last.then_inc(s_vtr, 1)

            def unit_start(it, i):
                if i % 2 == 0:
                    pe.wait_ge(s_wlo, N_AIN + 4 * it + i // 2 + 1)
                if i < 2:
                    if counted(4 * it - 1 + i):
                        pe.wait_ge(s_vz, 4 * it - 1 + i)
                elif i < 6:
                    pe.wait_ge(s_qkraw, 4 * it + i - 1)
                else:
                    pe.wait_ge(s_vz, 4 * it + i - 5)

            def piece(it, i, p):
                if p == 0:
                    unit_start(it, i)
                last = unit_part((N_AIN + i // 2) % 2, B_PROJ + i % 2, i % 2, range(2 * p, 2 * p + 2),
                                 h_hi, h_lo)
                if p == 3:
                    last.then_inc(s_unit, 1)

            def iteration(it, proj, att):
                for i in range(8):
                    if att:
                        scores(it, i, 0)
                    if att and i == 7:
                        scores(it, i, 1)
                    if proj and i == 7:
                        pe.wait_ge(s_vz, 4 * it + 2)
                        pe.wait_ge(s_qkn, 4 * it + 4)
                    if att and i == 1:
                        pe.wait_ge(s_vlo, 2 * it - 1)
                    if proj:
                        piece(it, i, 0)
                    if proj and i == 7:
                        transpose_v(0)
                    if att and i == 1:
                        transpose_v(1)
                    if i < 7:
                        if proj:
                            piece(it, i, 1)
                        if att:
                            scores(it, i, 1)
                    chunks = STEPS[i - 1][1] + 1 if att and i else 0
                    for c in range(min(2, chunks)):
                        transpose_p(it, i - 1, c)
                    if i == 7:
                        if proj:
                            piece(it, i, 1)
                    if proj:
                        piece(it, i, 2)
                    for c in range(min(2, chunks)):
                        pv(it, i - 1, c)
                        if c + 2 < chunks:
                            transpose_p(it, i - 1, c + 2)
                    if att and i == 7:
                        transpose_p(it, 7, 0)
                    if proj:
                        piece(it, i, 3)
                    for c in range(2, chunks):
                        pv(it, i - 1, c)
                    if att and i == 7:
                        pv(it, 7, 0)
                    if proj and 1 <= i <= 4:
                        head_square(it, i - 1)

            pe.wait_ge(s_msr, 4)
            pe.wait_ge(s_f, 1)
            iteration(0, True, False)
            iteration(1, True, True)
            with pe.Fori(2, PAIRS) as it:
                iteration(it, True, True)
            iteration(PAIRS, False, True)

            pe.wait_ge(s_vz, 4 * PAIRS)
            pe.wait_ge(s_exp, 16 * PAIRS)
            for m in range(KT):
                pe.wait_ge(s_wlo, N_AOUT + m + 1)
                for h in range(2):
                    if counted(2 * m + h - 3):
                        pe.wait_ge(s_or, 2 * m + h - 3)
                    bank = (2 * m + h) % 4
                    unit_part((N_AOUT + m) % 2, bank, h, range(KT - 1), h_hi, h_lo,
                              s_y2l if m == 0 else None, 1, 1)
                    if m == 0:
                        pe.wait_ge(s_y2l, KT + h)
                    unit_part((N_AOUT + m) % 2, bank, h, [KT - 1], h_hi, h_lo).then_inc(s_unit, 1)

        @block.scalar
        def _(act):
            A = nc.scalar.activation

            def split_w(n, slot, turn):
                act.wait_ge(s_wraw[slot], 16 * turn + 16)
                if counted(2 * n - 2):
                    act.wait_ge(s_unit, 2 * n - 2)
                A(w_hi[:, slot, :, :], w_raw[:, slot, :, :], ACT.Copy).then_inc(s_whi, 1)

            act.dma_start(g1[:, :], conv_gain).then_inc(s_const, 16)
            act.dma_start(taps[:, :, :], conv_taps).then_inc(s_const, 16)
            act.dma_start(g2[:, :], attn_gain).then_inc(s_const, 16)
            for side in range(2):
                r = slice(DH * side, DH * side + DH)
                act.dma_start(gq[r, :], q_gain).then_inc(s_const, 16)
                act.dma_start(gk[r, :], k_gain).then_inc(s_const, 16)
            act.dma_start(b_f[:, :], b_forget).then_inc(s_const, 16)

            for c in range(2 * KT):
                h, k = divmod(c, KT)
                if k % 4 == 0:
                    act.wait_ge(s_x[2 * h + k // 4], 16)
                if counted(c - 1):
                    act.wait_ge(s_sqa, c - 1)
                A(sq2[:, (c % 2) * HALF:(c % 2 + 1) * HALF], x_t[:, k, halves(h)], ACT.Square).then_inc(s_sqm, 1)
                if c == 4:
                    split_w(0, 0, 0)

            def rsqrt_guess(turn):
                act.wait_ge(s_msr, 2 * turn + 2)
                A(inv[:, :], mbuf, ACT.Ln).then_inc(s_rs0, 1)
                act.wait_ge(s_rs0, 2 * turn + 1)
                A(inv[:, :], inv[:, :], ACT.Exp, scale=-0.5).then_inc(s_rs0, 1)

            rsqrt_guess(0)

            def conv_block(j):
                for t in range(4):
                    split_w(4 * j + t + 1, (t + 1) % 2, 2 * j + (t + 1) // 2)
                    for h in range(2):
                        if t == 2:
                            act.wait_ge(s_evac, 8 * j + 4 + h + 1)
                            A(gate[:, halves(h)], gate[:, halves(h)], ACT.Silu).then_inc(s_gate, 1)
                        if t == 3:
                            act.wait_ge(s_y, 2 * j + h + 1)
                            A(y_hi[:, j, halves(h)], yb[:, halves(h)], ACT.Copy)\
                                .then_inc(s_yhi, 1)

            conv_block(0)
            with act.Fori(1, KT) as j:
                conv_block(j)

            with act.Fori(0, 2) as i:
                for t in range(4):
                    split_w(N_COUT + 4 * i + t + 1, (t + 1) % 2, 2 * KT + 2 * i + (t + 1) // 2)
                    for h in range(2):
                        u = 8 * i + 2 * t + h
                        act.wait_ge(s_evac, 8 * KT + u + 1)
                        act.wait_ge(s_sqa, 2 * KT + u - 1)
                        A(sq2[:, halves(h)], x_t[:, 4 * i + t, halves(h)], ACT.Square)\
                            .then_inc(s_sqm, 1)

            rsqrt_guess(1)
            split_w(N_AIN, 1, N_AIN // 2)
            f = p_big[0:NH, 0, :]
            act.wait_ge(s_f, 3)
            A(f, f, ACT.Exp).then_inc(s_fa, 1)
            act.wait_ge(s_fa, 1)
            A(f, f, ACT.Ln, bias=1.0).then_inc(s_fa, 1)
            act.wait_ge(s_f, 5)
            A(pt_hi[0:NH, :, :], f.rearrange("p (a n) -> p a n", a=2), ACT.Copy).then_inc(s_fa, 1)
            act.wait_ge(s_fa, 3)
            act.wait_ge(s_f, 6)
            A(v_st[0:NH, 0, :, :], pt_hi[0:NH, :, :].bitcast(F32).rearrange("p a n -> p (a n)"),
              ACT.Copy, scale=-1.0).then_inc(s_fa, 1)
            A(v_st[0:NH, 1, :, :], pt_lo[0:NH, :, :].bitcast(F32).rearrange("p a n -> p (a n)"),
              ACT.Copy, scale=-1.0).then_inc(s_fa, 1)

            def softmax_exp(it, i, par):
                pair = it - 1
                t = STEPS[i][1]
                w = 2 * P * (t + 1)
                col = 2 * (i % 2) + par
                act.wait_ge(s_max, 16 * pair + 2 * i + par + 1)
                if counted(CHUNKS * pair + (CHUNK0[i - 1] if i else 0) - (1 if i == 0 else 0)):
                    act.wait_ge(s_ptr, CHUNKS * pair + (CHUNK0[i - 1] if i else 0) - (1 if i == 0 else 0))
                if counted(16 * pair + 2 * i + par - 3):
                    act.wait_ge(s_rd, 16 * pair + 2 * i + par - 3)
                dst = (p_big if i % 2 == 0 else p_small)[:, par, 0:w]
                if t >= 2:
                    src = ps[:, B_SCORE:B_SCORE + 2, 0:w // 2]
                    dst = dst.rearrange("p (b n) -> p b n", b=2)
                else:
                    src = ps[:, B_SCORE + par, 0:w]
                A(dst, src, ACT.Exp, bias=neg_max[:, col:col + 1],
                  accum_out=denom[:, col:col + 1]).then_inc(s_exp, 1)

            def pt_split(it, g):
                pair = it - 1
                act.wait_ge(s_ptr, CHUNKS * pair + g + 1)
                if counted(CHUNKS * pair + g - 1):
                    act.wait_ge(s_pv, CHUNKS * pair + g - 1)
                A(pt_hi[:, g % 2, :], ps[:, B_PT + g % 2, :], ACT.Copy).then_inc(s_pth, 1)

            def out_copy(it, i):
                pair = it - 1
                side, t = STEPS[i]
                r = DH * side
                act.wait_ge(s_pv, CHUNKS * pair + CHUNK0[i] + t + 1)
                if counted(4 * pair + 2 * side + (0 if t == 2 else 1)):
                    act.wait_ge(s_y2, 4 * pair + 2 * side + (0 if t == 2 else 1))
                A(osum[r:r + DH, :], ps[DH:P, B_OUT, :], ACT.Copy).then_inc(s_oc, 1)

            def stack_hi(pair, side):
                own = slice(DH * side, DH * side + DH)
                other = slice(DH * (1 - side), DH * (1 - side) + DH)
                act.wait_ge(s_qkn, 4 * pair + 4)
                if counted(16 * pair - 8 + 8 * side):
                    act.wait_ge(s_sc, 16 * pair - 8 + 8 * side)
                act.wait_ge(s_clear, 1)
                A(q1[own, side, :], qn[own, :], ACT.Copy)
                A(q2[own, side, :], qn[own, :], ACT.Copy)
                A(k1[own, side, :], kn[own, :], ACT.Copy)
                A(k1[other, side, :], kn[own, :], ACT.Copy).then_inc(s_sthi, 1)

            def v_split(pair, side):
                act.wait_ge(s_vtr, 2 * pair + side + 1)
                if counted(CHUNKS * pair - 10 + 10 * side):
                    act.wait_ge(s_pv, CHUNKS * pair - 10 + 10 * side)
                act.wait_ge(s_cst, 64)
                A(v_st[:, side, :, 0:DH], ps[:, B_MISC, :].rearrange("p (k d) -> p k d", d=DH),
                  ACT.Copy).then_inc(s_vhi, 1)

            def iteration(it, proj, att):
                for i in range(8):
                    if att:
                        softmax_exp(it, i, 0)
                    if proj and 2 <= i <= 5:
                        u = i - 2
                        act.wait_ge(s_ssq, 4 * it + u + 1)
                        A(y0, ps[:, B_MISC, :], ACT.Ln, bias=eps_col[:, :]).then_inc(s_guess, 1)
                        act.wait_ge(s_guess, 8 * it + 2 * u + 1)
                        A(y0, y0, ACT.Exp, scale=-0.5).then_inc(s_guess, 1)
                    if att and i and i < 7:
                        for c in range(min(2, STEPS[i - 1][1] + 1)):
                            pt_split(it, CHUNK0[i - 1] + c)
                    if att:
                        softmax_exp(it, i, 1)
                    if proj and i % 2 == 0:
                        n = N_AIN + 4 * it + i // 2 + 1
                        split_w(n, (N_AIN + i // 2 + 1) % 2, 2 * it + (N_AIN + i // 2 + 1) // 2)
                    if att and i:
                        for c in range(2 if i < 7 else 0, STEPS[i - 1][1] + 1):
                            pt_split(it, CHUNK0[i - 1] + c)
                        if STEPS[i - 1][1] % 2 == 0:
                            out_copy(it, i - 1)
                    if att and i == 0:
                        stack_hi(it - 1, 1)
                    if att and i == 1:
                        v_split(it - 1, 1)
                    if proj and 1 <= i <= 4:
                        u = i - 1
                        act.wait_ge(s_qkraw, 4 * it + u + 1)
                        if counted(4 * it + u):
                            act.wait_ge(s_qkn, 4 * it + u)
                        if u == 0:
                            if counted(2 * it):
                                act.wait_ge(s_gz, 2 * it)
                        A(sq, (qn, kn)[u // 2][:, halves(u % 2)], ACT.Square).then_inc(s_qsq, 1)
                    if proj and i == 6:
                        stack_hi(it, 0)
                    if proj and i == 7:
                        v_split(it, 0)
                        z_exp(it, 0)
                    if att and not proj and i < 7:
                        y2_split(i, None)
                if proj:
                    z_exp(it, 1)
                if att:
                    pt_split(it, CHUNK0[7])
                    out_copy(it, 7)

            def z_exp(it, h):
                act.wait_ge(s_vz, 4 * it + 3 + h)
                if counted(2 * it + h):
                    act.wait_ge(s_gz, 2 * it + h)
                A(sq, y2[:, it, halves(h)], ACT.Exp, scale=-1.0).then_inc(s_ze, 1)

            def y2_split(k, h):
                cols = slice(0, S) if h is None else halves(h)
                act.wait_ge(s_unit, 2 * N_AOUT)
                act.wait_ge(s_y2, 4 * k + 4)
                A(h_hi[:, k, cols], y2[:, k, cols], ACT.Copy).then_inc(s_y2h, 1)

            iteration(0, True, False)
            iteration(1, True, True)
            with act.Fori(2, PAIRS) as it:
                iteration(it, True, True)
            iteration(PAIRS, False, True)
            y2_split(KT - 1, 0)
            y2_split(KT - 1, 1)

            for m in range(KT):
                if m + 1 < KT:
                    n = N_AOUT + m + 1
                    split_w(n, n % 2, n // 2)
        @block.vector
        def _(dve):
            v = nc.vector
            TT, TS, STT = v.tensor_tensor, v.tensor_scalar, v.scalar_tensor_tensor
            steps = [0]

            def own(ins):
                steps[0] += 1
                ins.then_inc(s_dve, 1)
                dve.wait_ge(s_dve, steps[0])

            v.memset(mean_d[:, :], 1.0 / D)
            v.memset(eps_col[:, :], EPS)
            for a in range(2):
                for b in range(2):
                    v.memset(mean_h[a * DH:(a + 1) * DH, b * DH:(b + 1) * DH], 1.0 / DH if a == b else 0.0)
            v.memset(mask_bf[:, 0:P], 0.0)
            v.memset(mask_bf[:, P:2 * P], MASKED).then_inc(s_vconst, 1)
            dve.wait_ge(s_const, 16 * 8)
            own(TS(gq[:, :], gq[:, :], -0.5 / DH ** 0.5, None, ALU.mult))
            own(TS(gk[:, :], gk[:, :], -0.5, None, ALU.mult))
            for c in range(2 * KT):
                h, k = divmod(c, KT)
                if k % 4 == 0:
                    dve.wait_ge(s_x[2 * h + k // 4], 16)
                own(TS(h_hi[:, k, halves(h)], x_t[:, k, halves(h)], g1[:, k:k + 1], None, ALU.mult))
                STT(h_lo[:, k, halves(h)], x_t[:, k, halves(h)], g1[:, k:k + 1],
                    h_hi[:, k, halves(h)].bitcast(F32), ALU.mult, ALU.subtract).then_inc(s_h, 1)

            def rsqrt(turn, banks):
                for h in range(2):
                    dve.wait_ge(s_ms, 2 * turn + h + 1)
                    TS(mbuf[:, halves(h)], ps[:, banks + h, :], EPS, None, ALU.add).then_inc(s_msr, 1)
                dve.wait_ge(s_rs0, 2 * turn + 2)
                t = ubuf[:, 0:S]
                own(TT(t, inv[:, :], inv[:, :], ALU.mult))
                own(STT(t, t, -0.5, mbuf, ALU.mult, ALU.mult))
                own(STT(inv[:, :], t, 1.5, inv[:, :], ALU.add, ALU.mult))
                return v.memset(ubuf[:, 0:2], 0.0).then_inc(s_inv, 1)

            rsqrt(0, 4)
            dve.wait_ge(s_inv, 1)

            with dve.Fori(0, KT) as j:
                base = steps[0] + j * 8
                local = 0
                for t in range(4):
                    for h in range(2):
                        u = 2 * t + h
                        hs = halves(h)
                        dve.wait_ge(s_unit, 8 * j + u + 1)
                        if t == 0:
                            TT(ca[:, hs], ps[:, u, :], inv[:, hs], ALU.mult).then_inc(s_evac, 1)
                        if t == 1:
                            dve.wait_ge(s_evac, 8 * j + h + 1)
                            TT(ubuf[:, 2 + h * HALF:2 + (h + 1) * HALF], ps[:, u, :], ca[:, hs],
                               ALU.mult).then_inc(s_evac, 1)
                            dve.wait_ge(s_u, 2 * j + h + 1)
                            for i in range(TAPS):
                                w = taps[:, TAPS - 1 - i, bass.ds(j, 1)]
                                us = ubuf[:, 2 + h * HALF - i:2 + (h + 1) * HALF - i]
                                if i == 0:
                                    ins = TS(ca[:, hs], us, w, None, ALU.mult)
                                else:
                                    ins = STT(ca[:, hs], us, w, ca[:, hs], ALU.mult, ALU.add)
                                local += 1
                                ins.then_inc(s_dve, 1)
                                dve.wait_ge(s_dve, base + local)
                        if t == 2:
                            TT(gate[:, hs], ps[:, u, :], inv[:, hs], ALU.mult).then_inc(s_evac, 1)
                        if t == 3:
                            TT(yb[:, hs], ps[:, u, :], inv[:, hs], ALU.mult).then_inc(s_evac, 1)
                            dve.wait_ge(s_evac, 8 * j + u + 1)
                            local += 1
                            TT(yb[:, hs], yb[:, hs], ca[:, hs], ALU.mult).then_inc(s_dve, 1)
                            dve.wait_ge(s_dve, base + local)
                            dve.wait_ge(s_gate, 2 * j + h + 1)
                            TT(yb[:, hs], yb[:, hs], gate[:, hs], ALU.mult).then_inc(s_y, 1)
                            dve.wait_ge(s_yhi, 2 * j + h + 1)
                            TT(y_lo[:, j, hs], yb[:, hs],
                               y_hi[:, j, hs].bitcast(F32), ALU.subtract).then_inc(s_ylo, 1)
                assert local == 8
            steps[0] += 8 * KT

            with dve.Fori(0, 2) as i:
                base = steps[0] + i * 8
                for t in range(4):
                    for h in range(2):
                        u = 2 * t + h
                        hs = halves(h)
                        m = 4 * i + t
                        gain = g2[:, bass.ds(m, 1)]
                        dve.wait_ge(s_unit, 8 * KT + 8 * i + u + 1)
                        TT(x_t[:, m, hs], ps[:, u, :], x_t[:, m, hs], ALU.add).then_inc(s_evac, 1)
                        dve.wait_ge(s_evac, 8 * KT + 8 * i + u + 1)
                        TS(h_hi[:, m, hs], x_t[:, m, hs], gain, None, ALU.mult).then_inc(s_dve, 1)
                        dve.wait_ge(s_dve, base + u + 1)
                        STT(h_lo[:, m, hs], x_t[:, m, hs], gain, h_hi[:, m, hs].bitcast(F32),
                            ALU.mult, ALU.subtract).then_inc(s_h, 1)
            steps[0] += 16

            rsqrt(1, 2)
            dve.wait_ge(s_inv, 2)
            dve.wait_ge(s_spill, 16 * KT)
            f, m0, ones = p_big[0:NH, 0, :], p_big[0:NH, 1, :], kn[0:NH, :]
            v.memset(ones, 1.0)
            for h in range(2):
                dve.wait_ge(s_unit, 2 * N_FORGET + h + 1)
                ins = TT(f[:, halves(h)], ps[0:NH, h, :], inv[0:NH, halves(h)], ALU.mult)
            ins.then_inc(s_f, 1)
            dve.wait_ge(s_f, 1)
            own(TS(f, f, b_f[:, :], None, ALU.add))
            TS(m0, f, 0.0, None, ALU.min).then_inc(s_f, 1)
            dve.wait_ge(s_f, 2)
            STT(f, m0, 2.0, f, ALU.mult, ALU.subtract).then_inc(s_f, 1)
            dve.wait_ge(s_fa, 2)
            TT(m0, m0, f, ALU.subtract).then_inc(s_f, 1)
            dve.wait_ge(s_f, 4)
            v.tensor_tensor_scan(f, ones, m0, 0.0, ALU.mult, ALU.add).then_inc(s_f, 1)
            dve.wait_ge(s_fa, 3)
            TT(pt_lo[0:NH, :, :].rearrange("p a n -> p (a n)"), f,
               pt_hi[0:NH, :, :].bitcast(F32).rearrange("p a n -> p (a n)"), ALU.subtract).then_inc(s_f, 1)

            def row_max(it, i, par):
                pair = it - 1
                t = STEPS[i][1]
                w = 2 * P * (t + 1)
                col = 2 * (i % 2) + par
                dve.wait_ge(s_sc, 16 * pair + 2 * i + par + 1)
                if t >= 2:
                    src, ax = ps[:, B_SCORE:B_SCORE + 2, 0:w // 2], AX.XY
                else:
                    src, ax = ps[:, B_SCORE + par, 0:w], AX.X
                v.tensor_reduce(neg_max[:, col:col + 1], src, ax, ALU.max, negate=True).then_inc(s_max, 1)

            def invert(it, i, par):
                pair = it - 1
                col = 2 * (i % 2) + par
                dve.wait_ge(s_exp, 16 * pair + 2 * i + par + 1)
                if counted(16 * pair + 2 * i + par - 3):
                    dve.wait_ge(s_pn, 16 * pair + 2 * i + par - 3)
                v.reciprocal(rdenom[:, col:col + 1], denom[:, col:col + 1]).then_inc(s_rd, 1)

            def pt_low(it, g):
                pair = it - 1
                dve.wait_ge(s_pth, CHUNKS * pair + g + 1)
                TT(pt_lo[:, g % 2, :], ps[:, B_PT + g % 2, :], pt_hi[:, g % 2, :].bitcast(F32),
                   ALU.subtract).then_inc(s_ptl, 1)

            def out_gate(it, i):
                pair = it - 1
                side, t = STEPS[i]
                r = DH * side
                k = 4 * pair + 2 * side + (1 if t == 2 else 2)
                cols = halves(1 if t == 2 else 0)
                dve.wait_ge(s_oc, k)
                TT(osum[r:r + DH, :], ps[0:DH, B_OUT, :], osum[r:r + DH, :], ALU.add).then_inc(s_os, 1)
                dve.wait_ge(s_os, k)
                dve.wait_ge(s_gz, 2 * pair + 2)
                dst = y2[r:r + DH, pair, cols]
                TT(dst, osum[r:r + DH, :], dst, ALU.mult).then_inc(s_y2, 1)

            def stack_q_lo(pair, side):
                o, r = DH * side, DH * (1 - side)
                dve.wait_ge(s_sthi, 2 * pair + side + 1)
                TT(q1[r:r + DH, side, :], qn[o:o + DH, :], q1[o:o + DH, side, :].bitcast(F32),
                   ALU.subtract).then_inc(s_stq, 1)

            def v_low(pair, side):
                dve.wait_ge(s_vhi, 2 * pair + side + 1)
                TT(v_st[:, side, :, DH:P], ps[:, B_MISC, :].rearrange("p (k d) -> p k d", d=DH),
                   v_st[:, side, :, 0:DH].bitcast(F32), ALU.subtract).then_inc(s_vlo, 1)

            NEWTON = 3

            def iteration(it, proj, att, base):
                local = 0
                for i in range(8):
                    if att:
                        row_max(it, i, 0)
                        if i == 7:
                            row_max(it, i, 1)
                    if proj and 1 <= i <= 4:
                        u = i - 1
                        dve.wait_ge(s_unit, 2 * N_AIN + 8 * it + u + 1)
                        if u < 2:
                            if counted(2 * it):
                                dve.wait_ge(s_stq, 2 * it)
                        if counted(2 * it):
                            dve.wait_ge(s_stk, 2 * it)
                        TT((qn, kn)[u // 2][:, halves(u % 2)], ps[:, B_PROJ + u % 2, :],
                           inv[:, halves(u % 2)], ALU.mult).then_inc(s_qkraw, 1)
                    if att and i:
                        for c in range(min(2, STEPS[i - 1][1] + 1)):
                            pt_low(it, CHUNK0[i - 1] + c)
                    if att:
                        if i < 7:
                            row_max(it, i, 1)
                        invert(it, i, 0)
                    if att and i:
                        for c in range(2, STEPS[i - 1][1] + 1):
                            pt_low(it, CHUNK0[i - 1] + c)
                    if att:
                        invert(it, i, 1)
                    if att and i and STEPS[i - 1][1] % 2 == 0:
                        out_gate(it, i - 1)
                    if proj and 2 <= i <= 5:
                        u = i - 2
                        dst = (qn, kn)[u // 2][:, halves(u % 2)]
                        dve.wait_ge(s_guess, 8 * it + 2 * u + 2)
                        TT(sq, y0, y0, ALU.mult).then_inc(s_dve, 1)
                        dve.wait_ge(s_dve, base + local + 1)
                        STT(sq, ps[:, B_MISC, :], EPS, sq, ALU.add, ALU.mult).then_inc(s_dve, 1)
                        dve.wait_ge(s_dve, base + local + 2)
                        STT(sq, sq, 3.0, y0, ALU.subtract, ALU.mult).then_inc(s_dve, 1)
                        dve.wait_ge(s_dve, base + local + 3)
                        local += NEWTON
                        STT(dst, dst, (gq, gk)[u // 2][:, :], sq, ALU.mult, ALU.mult).then_inc(s_qkn, 1)
                    if proj and 5 <= i <= 7:
                        vz_evac(it, i - 1)
                    if att and i == 0:
                        stack_q_lo(it - 1, 1)
                    if att and i == 1:
                        v_low(it - 1, 1)
                    if proj and i == 6:
                        stack_q_lo(it, 0)
                    if proj and i == 7:
                        v_low(it, 0)
                        local = z_gate(it, 0, base, local)
                if proj:
                    vz_evac(it, 7)
                    local = z_gate(it, 1, base, local)
                if att:
                    pt_low(it, CHUNK0[7])
                    out_gate(it, 7)
                return local

            def vz_evac(it, u):
                h = u % 2
                dve.wait_ge(s_unit, 2 * N_AIN + 8 * it + u + 1)
                if u < 6:
                    if counted(2 * it):
                        dve.wait_ge(s_vtr, 2 * it)
                    dst = v_t[:, halves(h)]
                else:
                    dst = y2[:, it, halves(h)]
                TT(dst, ps[:, B_PROJ + h, :], inv[:, halves(h)], ALU.mult).then_inc(s_vz, 1)

            def z_gate(it, h, base, local):
                dve.wait_ge(s_ze, 2 * it + h + 1)
                TS(sq, sq, 1.0, None, ALU.add).then_inc(s_dve, 1)
                dve.wait_ge(s_dve, base + local + 1)
                v.reciprocal(sq, sq).then_inc(s_dve, 1)
                dve.wait_ge(s_dve, base + local + 2)
                dst = y2[:, it, halves(h)]
                TT(dst, dst, sq, ALU.mult).then_inc(s_gz, 1)
                return local + 2

            for side in range(2):
                r = DH * (1 - side)
                for st in (q2, k2):
                    own(v.memset(st[r:r + DH, side, :].bitcast(F32), 0.0))
            for side in range(2):
                r = DH * (1 - side)
                for st in (q2, k2):
                    ins = v.memset(st[r:r + 4, side, :].bitcast(F32), 1.0)
            ins.then_inc(s_clear, 1)
            dve.wait_ge(s_cst, 64)
            per = iteration(0, True, False, steps[0])
            per = iteration(1, True, True, steps[0] + per)
            with dve.Fori(2, PAIRS) as it:
                iteration(it, True, True, steps[0] + it * per)
            iteration(PAIRS, False, True, 0)

            for m in range(KT):
                for h in range(2):
                    dve.wait_ge(s_unit, 2 * (N_AOUT + m) + h + 1)
                    dve.wait_ge(s_x1r[m % 2], 16 * (m // 2 + 1))
                    if counted(16 * (m // 2)):
                        dve.wait_ge(s_out[2 * (m % 2) + h], 16 * (m // 2))
                    TT(p_big[:, m % 2, halves(h)], ps[:, (2 * m + h) % 4, :],
                       (qn, kn)[m % 2][:, halves(h)], ALU.add).then_inc(s_or, 1)

        @block.gpsimd
        def _(pool):
            g = nc.gpsimd
            TT = g.tensor_tensor
            g.memset(ident[:, :], 0.0).then_inc(s_ident, 1)
            pool.wait_ge(s_ident, 1)
            g.affine_select(out=ident[:, :], in_=ident[:, :], compare_op=ALU.not_equal, fill=1.0, base=0,
                            pattern=[[-1, P]], channel_multiplier=1).then_inc(s_ident, 1)
            g.memset(acc, 0.0).then_inc(s_zero, 1)
            pool.wait_ge(s_zero, 1)
            pool.wait_ge(s_vconst, 1)
            pool.wait_ge(s_ident, 2)
            g.affine_select(out=mask_bf[:, 0:P], in_=mask_bf[:, 0:P], compare_op=ALU.is_ge, fill=MASKED,
                            base=0, pattern=[[-1, P]], channel_multiplier=1)
            g.tensor_copy(ident_bf[:, :], ident[:, :]).then_inc(s_ident, 1)

            def w_low(n, slot):
                pool.wait_ge(s_whi, n + 1)
                TT(w_lo[:, slot, :, :], w_raw[:, slot, :, :], w_hi[:, slot, :, :].bitcast(F32),
                   ALU.subtract).then_inc(s_wlo, 1)

            def add_square(k, c, h):
                pool.wait_ge(s_sqm, c + 1)
                if counted(c):
                    pool.wait_ge(s_sqa, c)
                TT(acc[:, halves(h)], acc[:, halves(h)], sq2[:, (c % 2) * HALF:(c % 2 + 1) * HALF],
                   ALU.add).then_inc(s_sqa, 1)

            for c in range(2 * KT):
                add_square(c % KT, c, c // KT)
                if c == 3:
                    w_low(0, 0)

            with pool.Fori(0, KT) as j:
                for t in range(4):
                    w_low(4 * j + t + 1, (t + 1) % 2)
                    if t == 1:
                        for h in range(2):
                            pool.wait_ge(s_evac, 8 * j + 2 + h + 1)
                            pool.wait_ge(s_inv, 1)
                            us = ubuf[:, 2 + h * HALF:2 + (h + 1) * HALF]
                            TT(us, us, inv[:, halves(h)], ALU.mult).then_inc(s_u, 1)

            pool.wait_ge(s_ylo, 2 * KT)
            g.memset(acc, 0.0).then_inc(s_zero, 1)
            pool.wait_ge(s_zero, 2)
            with pool.Fori(0, 2) as i:
                for t in range(4):
                    w_low(N_COUT + 4 * i + t + 1, (t + 1) % 2)
                    for h in range(2):
                        c = 2 * KT + 8 * i + 2 * t + h
                        pool.wait_ge(s_sqm, c + 1)
                        pool.wait_ge(s_sqa, c)
                        TT(acc[:, halves(h)], acc[:, halves(h)], sq2[:, halves(h)], ALU.add)\
                            .then_inc(s_sqa, 1)
            w_low(N_AIN, 1)

            def normalise(it, i, par):
                pair = it - 1
                w = 2 * P * (STEPS[i][1] + 1)
                col = 2 * (i % 2) + par
                pool.wait_ge(s_rd, 16 * pair + 2 * i + par + 1)
                p = (p_big if i % 2 == 0 else p_small)[:, par, 0:w]
                TT(p, p, rdenom[:, col:col + 1].broadcast_to([P, w]), ALU.mult).then_inc(s_pn, 1)

            def stack_k_lo(pair, side):
                r = DH * side
                pool.wait_ge(s_sthi, 2 * pair + side + 1)
                TT(k2[r:r + DH, side, :], kn[r:r + DH, :], k1[r:r + DH, side, :].bitcast(F32),
                   ALU.subtract).then_inc(s_stk, 1)
                pool.wait_ge(s_stk, 2 * pair + side + 1)

            def y2_low(k, cols):
                pool.wait_ge(s_y2h, k)
                TT(h_lo[:, min(k - 1, KT - 1), cols], y2[:, min(k - 1, KT - 1), cols],
                   h_hi[:, min(k - 1, KT - 1), cols].bitcast(F32), ALU.subtract).then_inc(s_y2l, 1)

            def iteration(it, proj, att):
                for i in range(8):
                    if att:
                        normalise(it, i, 0)
                        normalise(it, i, 1)
                    if proj and i % 2 == 0:
                        w_low(N_AIN + 4 * it + i // 2 + 1, (N_AIN + i // 2 + 1) % 2)
                    if att and i == 0:
                        pool.wait_ge(s_pn, 16 * it - 14)
                        if proj:
                            pool.wait_ge(s_wlo, N_AIN + 4 * it + 2)
                        stack_k_lo(it - 1, 1)
                    if proj and i == 6:
                        if att:
                            pool.wait_ge(s_pn, 16 * it - 2)
                        pool.wait_ge(s_wlo, N_AIN + 4 * it + 5)
                        stack_k_lo(it, 0)
                    if att and not proj and i < 7:
                        y2_low(i + 1, slice(0, S))

            iteration(0, True, False)
            iteration(1, True, True)
            with pool.Fori(2, PAIRS) as it:
                iteration(it, True, True)
            iteration(PAIRS, False, True)
            y2_low(KT, halves(0))
            y2_low(KT + 1, halves(1))
            for m in range(KT - 1):
                w_low(N_AOUT + m + 1, (N_AOUT + m + 1) % 2)


def kernel(**inputs):
    import numpy as np
    import concourse.bacc as bacc
    from concourse.bass_utils import run_bass_kernel_spmd

    nc = bacc.Bacc("TRN2", target_bir_lowering=False, num_devices=1)

    def tiles(w, blocks, order):
        w = w.reshape(KT, P, blocks, KT, P).transpose(3, 2, 1, 0, 4)[:, order]
        return w.reshape(KT * blocks, P, KT, P)

    def rows(v):
        return np.moveaxis(v.reshape(*v.shape[:-1], KT, P), -1, 0)

    w_a = inputs["attn_w_in"][0]
    laid_out = {
        "x": inputs["x"][0].T.reshape(KT, P, S).transpose(1, 0, 2),
        "w_cin": tiles(inputs["conv_w_in"][0], 4, CONV_COLUMNS),
        "w_cout": tiles(inputs["conv_w_out"][0], 1, [0]),
        "w_ain": tiles(w_a[:, :4 * D], 4, [0, 1, 2, 3]),
        "w_forget": w_a[:, 4 * D:].reshape(KT, P, NH).transpose(1, 0, 2),
        "w_aout": tiles(inputs["attn_w_out"][0], 1, [0]),
        "conv_gain": rows(inputs["conv_norm_g"][0]),
        "conv_taps": rows(inputs["conv_w"][0]),
        "attn_gain": rows(inputs["attn_norm_g"][0]),
        "b_forget": inputs["attn_b_f"][0].reshape(NH, 1),
        "q_gain": inputs["attn_q_norm_g"][0].reshape(DH, 1),
        "k_gain": inputs["attn_k_norm_g"][0].reshape(DH, 1),
    }
    arrays, args = {}, []
    for name, a in laid_out.items():
        a = np.ascontiguousarray(a)
        arrays[f"in_{name}"] = a
        args.append(nc.dram_tensor(f"in_{name}", a.shape, mybir.dt.from_np(a.dtype), kind="ExternalInput").ap())
    args.append(nc.dram_tensor("out", (P, KT, S), F32, kind="ExternalOutput").ap())
    hybrid(nc, *args)
    result = run_bass_kernel_spmd(nc, [arrays], core_ids=[0])
    return result.results[0]["out"].transpose(2, 1, 0).reshape(1, S, D)
```

```python
import concourse.bass as bass
from concourse import mybir
from contextlib import ExitStack

F32 = mybir.dt.float32
F32R = mybir.dt.float32r
BF16 = mybir.dt.bfloat16
ALU = mybir.AluOpType
ACT = mybir.ActivationFunctionType
AX = mybir.AxisListType

P = 128
D = 1024
S = 1024
KT = D // P
NH = 16
DH = D // NH
PAIRS = NH // 2
HALF = S // 2
TAPS = 3
EPS = 1e-6
MASKED = -3.0e38

N_CIN, N_COUT, N_FORGET, N_AIN, N_AOUT = 0, 4 * KT, 5 * KT, 5 * KT + 1, 9 * KT + 1
N_TILES = 10 * KT + 1
CONV_COLUMNS = [1, 2, 3, 0]
B_PROJ, B_SCORE, B_PT, B_OUT, B_MISC = 0, 2, 4, 6, 7
STEPS = [(x, t) for x in range(2) for t in (3, 2, 1, 0)]
CHUNK0 = [0, 4, 7, 9, 10, 14, 17, 19]
CHUNKS = 20


def counted(value):
    return not isinstance(value, int) or value > 0


def hybrid(nc, x, w_cin, w_cout, w_ain, w_forget, w_aout, conv_gain, conv_taps, attn_gain, b_forget,
           q_gain, k_gain, out):
    x1_dram = nc.dram_tensor("x1_dram", [P, KT, S], F32, kind="Internal").ap()
    c_dram = nc.dram_tensor("c_dram", [NH, 4, S], F32, kind="Internal").ap()

    with ExitStack() as ctx:
        def sb(name, shape, dt=F32, where=ctx):
            return where.enter_context(nc.sbuf_tensor(name, shape, dt))

        def sem(name):
            return ctx.enter_context(nc.semaphore(name))

        ps = ctx.enter_context(nc.psum_tensor("ps", [P, 8, HALF], F32))

        h_hi = sb("h_hi", [P, KT, S], F32R)
        h_lo = sb("h_lo", [P, KT, S], F32R)
        w_raw = sb("w_raw", [P, 2, KT, P])
        w_hi = sb("w_hi", [P, 2, KT, P], F32R)
        w_lo = sb("w_lo", [P, 2, KT, P], F32R)
        inv = sb("inv", [P, S])
        scr = sb("scr", [P, 3 * S])
        ubuf = sb("ubuf", [P, S + 8])
        ident = sb("ident", [P, P])
        ident_bf = sb("ident_bf", [P, P], BF16)
        mask_bf = sb("mask_bf", [P, 2 * P], BF16)
        mean_d = sb("mean_d", [P, P])
        mean_h = sb("mean_h", [P, P])
        g1 = sb("g1", [P, KT])
        g2 = sb("g2", [P, KT])
        taps = sb("taps", [P, TAPS, KT])
        gq = sb("gq", [P, 1])
        gk = sb("gk", [P, 1])
        b_f = sb("b_f", [NH, 1])
        eps_col = sb("eps_col", [P, 1])
        neg_max = sb("neg_max", [P, 4])
        denom = sb("denom", [P, 4])
        rdenom = sb("rdenom", [P, 4])

        acc = scr[:, 0:S]
        sq2 = scr[:, S:2 * S]
        mbuf = scr[:, 2 * S:3 * S]
        ca = scr[:, 0:S]
        gate = scr[:, S:2 * S]
        yb = scr[:, 2 * S:3 * S]
        sq = scr[:, 0:HALF]
        y0 = scr[:, HALF:S]
        osum = scr[:, S:S + HALF]
        p_small = scr[:, S + HALF:3 * S].rearrange("p (b n) -> p b n", b=2)
        v_t = ubuf[:, 0:S]
        newton = ubuf[:, HALF:S]

        conv_ctx = ExitStack()
        x_t = sb("x_t", [P, KT, S], where=conv_ctx)
        y_hi = sb("y_hi", [P, KT, S], F32R, where=conv_ctx)
        y_lo = sb("y_lo", [P, KT, S], F32R, where=conv_ctx)
        conv_ctx.close()

        y2 = sb("y2", [P, KT, S])
        q1 = sb("q1", [P, 2, S], F32R)
        k1 = sb("k1", [P, 2, S], F32R)
        q2 = sb("q2", [P, 2, S], F32R)
        k2 = sb("k2", [P, 2, S], F32R)
        qn = sb("qn", [P, S])
        kn = sb("kn", [P, S])
        v_st = sb("v_st", [P, 2, KT, P], F32R)
        p_big = sb("p_big", [P, 2, S])
        pt_hi = sb("pt_hi", [P, 2, HALF], F32R)
        pt_lo = sb("pt_lo", [P, 2, HALF], F32R)

        s_const = sem("const_landed")
        s_ident = sem("identity_made")
        s_vconst = sem("constants_made")
        s_x = [sem(f"x_landed{i}") for i in range(4)]
        s_wraw = [sem(f"w_landed{i}") for i in range(2)]
        s_whi = sem("w_hi_made")
        s_wlo = sem("w_lo_made")
        s_unit = sem("units_done")
        s_sqm = sem("squares_made")
        s_sqa = sem("squares_added")
        s_h = sem("h_ready")
        s_ms = sem("mean_square_done")
        s_msr = sem("mean_square_read")
        s_rs0 = sem("rsqrt_guessed")
        s_inv = sem("inv_ready")
        s_evac = sem("conv_units_evacuated")
        s_u = sem("u_scaled")
        s_gate = sem("gate_made")
        s_y = sem("y_made")
        s_yhi = sem("y_hi_made")
        s_ylo = sem("y_lo_made")
        s_spill = sem("x1_stored")
        s_clear = sem("stacks_cleared")
        s_f = sem("forget_steps")
        s_fa = sem("forget_act_steps")
        s_cst = sem("c_stored")
        s_crow = [sem(f"c_rows_landed{i}") for i in range(2)]
        s_qkraw = sem("qk_evacuated")
        s_vz = sem("vz_evacuated")
        s_qsq = sem("qk_squared")
        s_ssq = sem("head_square_done")
        s_guess = sem("head_rsqrt_guessed")
        s_qkn = sem("qk_normed")
        s_qhi = sem("stack_q_hi_made")
        s_khi = sem("stack_k_hi_made")
        s_stq = sem("stack_q_lo_made")
        s_stk = sem("stack_k_lo_made")
        s_vtr = sem("v_transposed")
        s_vhi = sem("v_hi_made")
        s_vlo = sem("v_lo_made")
        s_sc = sem("scores_done")
        s_max = sem("row_max_done")
        s_exp = sem("exp_done")
        s_rd = sem("denominators_inverted")
        s_pn = sem("p_normalised")
        s_ptr = sem("p_transposed")
        s_pth = sem("pt_hi_made")
        s_ptl = sem("pt_lo_made")
        s_pv = sem("pv_done")
        s_oc = sem("out_lo_half_copied")
        s_os = sem("out_halves_summed")
        s_y2 = sem("y2_made")
        s_ze = sem("z_exp_done")
        s_gz = sem("z_gate_made")
        s_y2h = sem("y2_hi_made")
        s_y2l = sem("y2_lo_made")
        s_x1r = [sem(f"x1_reloaded{i}") for i in range(2)]
        s_or = sem("out_residual_added")
        s_out = [sem(f"out_stored{i}") for i in range(4)]
        s_dve = sem("vector_steps")
        s_zero = sem("sums_cleared")

        block = ctx.enter_context(nc.Block())

        def halves(h):
            return slice(h * HALF, (h + 1) * HALF)

        @block.sync
        def _(sp):
            def load_w(src, n, slot, tile):
                if counted(n - 1):
                    sp.wait_ge(s_whi, n - 1)
                    sp.wait_ge(s_wlo, n - 1)
                sp.dma_start(w_raw[:, slot, :, :], src[tile]).then_inc(s_wraw[slot], 16)

            def load_x(i):
                h, ks = i // 2, slice(4 * (i % 2), 4 * (i % 2) + 4)
                sp.dma_start(x_t[:, ks, halves(h)], x[:, ks, halves(h)]).then_inc(s_x[i], 16)

            load_x(0)
            load_w(w_cin, 0, 0, 0)
            load_x(1)
            load_w(w_cin, 1, 1, 1)
            load_x(2)
            load_x(3)
            load_w(w_cin, 2, 0, 2)
            load_w(w_cin, 3, 1, 3)
            with sp.Fori(1, KT) as j:
                for t in range(4):
                    load_w(w_cin, 4 * j + t, t % 2, 4 * j + t)
            for m in range(KT + 3):
                if m < KT:
                    load_w(w_cout, N_COUT + m, m % 2, m)
                elif m == KT:
                    sp.wait_ge(s_whi, N_FORGET - 1)
                    sp.wait_ge(s_wlo, N_FORGET - 1)
                    sp.dma_start(w_raw[:, 0, :, 0:NH], w_forget).then_inc(s_wraw[0], 16)
                else:
                    load_w(w_ain, N_AIN + m - KT - 1, m % 2, m - KT - 1)
                if m >= 3:
                    sp.wait_ge(s_evac, 8 * KT + 2 * (m - 3) + 2)
                    sp.dma_start(x1_dram[:, m - 3, :], x_t[:, m - 3, :]).then_inc(s_spill, 16)
            sp.wait_ge(s_fa, 3)
            sp.dma_start(c_dram[:, 0, :], pt_hi[0:NH, :, :].bitcast(F32)).then_inc(s_cst, 16)
            sp.wait_ge(s_f, 6)
            sp.dma_start(c_dram[:, 1, :], pt_lo[0:NH, :, :].bitcast(F32)).then_inc(s_cst, 16)
            sp.wait_ge(s_fa, 4)
            sp.dma_start(c_dram[:, 2, :], v_st[0:NH, 0, :, :].bitcast(F32)).then_inc(s_cst, 16)
            sp.wait_ge(s_fa, 5)
            sp.dma_start(c_dram[:, 3, :], v_st[0:NH, 1, :, :].bitcast(F32)).then_inc(s_cst, 16)

            def c_rows(side, pair):
                own = P // 2 * (1 - side)
                head = 2 * pair + side
                sp.dma_start(q2[own:own + 2, side, :].bitcast(F32), c_dram[bass.ds(head, 1), 0:2, :]
                             .rearrange("a c s -> (a c) s")).then_inc(s_crow[side], 16)
                sp.dma_start(k2[own + 2:own + 4, side, :].bitcast(F32), c_dram[bass.ds(head, 1), 2:4, :]
                             .rearrange("a c s -> (a c) s")).then_inc(s_crow[side], 16)

            def iteration(it, proj, att):
                pair = it - 1
                if att:
                    if counted(16 * pair):
                        sp.wait_ge(s_sc, 16 * pair)
                    c_rows(1, pair)
                if proj:
                    n = N_AIN + 4 * it
                    for t in range(4):
                        m = n + 2 + t
                        if not isinstance(it, int) or 4 * it + t + 2 < 4 * PAIRS:
                            load_w(w_ain, m, (N_AIN + t) % 2, 4 * it + t + 2)
                        else:
                            load_w(w_aout, m, (N_AIN + t) % 2, t - 2)
                        if t == 2:
                            if counted(16 * pair + 8):
                                sp.wait_ge(s_sc, 16 * pair + 8)
                            if isinstance(it, int) and it == 0:
                                sp.wait_ge(s_cst, 64)
                                sp.wait_ge(s_clear, 1)
                            c_rows(0, it)

            iteration(0, True, False)
            iteration(1, True, True)
            with sp.Fori(2, PAIRS - 1) as it:
                iteration(it, True, True)
            iteration(PAIRS - 1, True, True)
            iteration(PAIRS, False, True)
            def store_out(m):
                for h in range(2):
                    sp.wait_ge(s_or, 2 * m + h + 1)
                    sp.dma_start(out[:, m, halves(h)], p_big[:, m % 2, halves(h)])\
                        .then_inc(s_out[2 * (m % 2) + h], 16)

            sp.wait_ge(s_spill, 16 * KT)
            for m in range(KT):
                if m >= 2:
                    load_w(w_aout, N_AOUT + m, (N_AOUT + m) % 2, m)
                sp.wait_ge(s_stk, 2 * PAIRS)
                sp.wait_ge(s_stq, 2 * PAIRS)
                sp.wait_ge(s_qhi, 2 * PAIRS)
                sp.wait_ge(s_khi, 2 * PAIRS)
                if counted(2 * (m - 2) + 2):
                    sp.wait_ge(s_or, 2 * (m - 2) + 2)
                sp.dma_start((qn, kn)[m % 2][:, :], x1_dram[:, m, :]).then_inc(s_x1r[m % 2], 16)
                if m >= 2:
                    store_out(m - 2)
            store_out(KT - 2)
            store_out(KT - 1)
            for i in range(4):
                sp.wait_ge(s_out[i], 16 * (KT // 2))

        @block.tensor
        def _(pe):
            mm = nc.tensor.matmul

            def unit_part(slot, bank, h, ks, mov_hi, mov_lo, ready=None, first=0, step=0):
                last = None
                for k in ks:
                    if ready is not None:
                        pe.wait_ge(ready, first + step * k)
                    for st, mov in ((w_hi, mov_hi), (w_hi, mov_lo), (w_lo, mov_hi)):
                        last = mm(ps[:, bank, :], st[:, slot, k, :], mov[:, k, halves(h)],
                                  start=(k == 0 and st is w_hi and mov is mov_hi),
                                  stop=(k == KT - 1 and st is w_lo))
                return last

            def mean_square(turn, banks):
                for h in range(2):
                    pe.wait_ge(s_sqa, turn * 2 * KT + 2 * KT - (1 - h) * (KT if turn == 0 else 1))
                    mm(ps[:, banks + h, :], mean_d[:, :], acc[:, halves(h)], start=True, stop=True)\
                        .then_inc(s_ms, 1)

            pe.wait_ge(s_vconst, 1)
            pe.wait_ge(s_ident, 3)
            mean_square(0, 4)

            def conv_block(j, first):
                for t in range(4):
                    n = 4 * j + t
                    pe.wait_ge(s_wlo, n + 1)
                    for h in range(2):
                        u = 2 * t + h
                        if first:
                            if t == 2:
                                pe.wait_ge(s_msr, h + 1)
                        else:
                            pe.wait_ge(s_evac, 8 * j + u - 7)
                        unit_part(t % 2, u, h, range(KT), h_hi, h_lo,
                                  s_h if first and t == 0 else None, KT * h + 1, 1).then_inc(s_unit, 1)

            conv_block(0, True)
            with pe.Fori(1, KT) as j:
                conv_block(j, False)

            with pe.Fori(0, 2) as i:
                for t in range(4):
                    pe.wait_ge(s_wlo, N_COUT + 4 * i + t + 1)
                    for h in range(2):
                        u = 2 * t + h
                        pe.wait_ge(s_evac, 8 * KT + 8 * i + u - 7)
                        unit_part(t % 2, u, h, range(KT), y_hi, y_lo,
                                  s_ylo if t == 0 else None, h + 1, 2).then_inc(s_unit, 1)

            pe.wait_ge(s_wlo, N_FORGET + 1)
            for h in range(2):
                pe.wait_ge(s_evac, 10 * KT - 8 + h + 1)
                unit_part(0, h, h, range(KT), h_hi, h_lo,
                          s_h, 2 * KT + h + 1, 2).then_inc(s_unit, 1)
            pe.wait_ge(s_evac, 10 * KT)
            mean_square(1, 2)

            def scores(it, i, par):
                pair = it - 1
                side, t = STEPS[i]
                if t == 3 and par == 0:
                    pe.wait_ge(s_qhi, 2 * pair + side + 1)
                    pe.wait_ge(s_khi, 2 * pair + side + 1)
                    pe.wait_ge(s_stq, 2 * pair + side + 1)
                    pe.wait_ge(s_stk, 2 * pair + side + 1)
                    pe.wait_ge(s_crow[side], 32 * pair + 32)
                if counted(16 * pair + 2 * i + (par if t >= 2 else 0 if t == 1 else par - 1)):
                    pe.wait_ge(s_exp, 16 * pair + 2 * i + (par if t >= 2 else 0 if t == 1 else par - 1))
                qs = (2 * t + par) * P
                n, w = (2, P * (t + 1)) if t >= 2 else (1, 2 * P * (t + 1))
                for c in range(n):
                    bank = B_SCORE + (c if t >= 2 else par)
                    last_c = c == n - 1
                    for a, b in ((q1, k1), (q2, k2)):
                        last = mm(ps[:, bank, 0:w], a[:, side, qs:qs + P], b[:, side, c * w:(c + 1) * w],
                                  start=(a is q1), stop=(a is q2 and not last_c))
                    if last_c:
                        lo = 2 * P * t - c * w + par * P
                        mw = 2 * P - par * P
                        last = mm(ps[:, bank, lo:lo + mw], ident_bf[:, :], mask_bf[:, 0:mw],
                                  start=False, stop=True)
                last.then_inc(s_sc, 1)

            def transpose_p(it, i, c):
                pair = it - 1
                t = STEPS[i][1]
                g = CHUNK0[i] + c
                if c == 0:
                    pe.wait_ge(s_pn, 16 * pair + 2 * i + 2)
                if counted(CHUNKS * pair + g - 1):
                    pe.wait_ge(s_ptl, CHUNKS * pair + g - 1)
                src = p_big if i % 2 == 0 else p_small
                for kp in range(2):
                    for par in range(2):
                        at = (2 * kp + par) * P
                        last = nc.tensor.transpose(ps[:, B_PT + g % 2, at:at + P],
                                                   src[:, par, (2 * c + kp) * P:(2 * c + kp + 1) * P],
                                                   ident[:, :])
                last.then_inc(s_ptr, 1)

            def pv(it, i, c):
                pair = it - 1
                side, t = STEPS[i]
                g = CHUNK0[i] + c
                if c == 0 and t % 2 == 1:
                    if counted(4 * pair + 2 * side + (0 if t == 3 else 1)):
                        pe.wait_ge(s_os, 4 * pair + 2 * side + (0 if t == 3 else 1))
                    pe.wait_ge(s_vlo, 2 * pair + side + 1)
                pe.wait_ge(s_ptl, CHUNKS * pair + g + 1)
                at = (t % 2) * 2 * P
                for kp in range(2):
                    for mov in (pt_hi, pt_lo):
                        last = mm(ps[:, B_OUT, at:at + 2 * P], v_st[:, side, 2 * c + kp, :],
                                  mov[:, g % 2, kp * 2 * P:(kp + 1) * 2 * P],
                                  start=(c == 0 and kp == 0 and mov is pt_hi),
                                  stop=(c == t and kp == 1 and mov is pt_lo))
                last.then_inc(s_pv, 1)

            def head_square(it, u):
                if u == 0:
                    if counted(2 * it):
                        pe.wait_ge(s_vlo, 2 * it)
                if counted(4 * it + u):
                    pe.wait_ge(s_qkn, 4 * it + u)
                pe.wait_ge(s_qsq, 4 * it + u + 1)
                mm(ps[:, B_MISC, :], mean_h[:, :], sq, start=True, stop=True).then_inc(s_ssq, 1)

            def transpose_v(side):
                r = DH * side
                for k in range(KT):
                    last = nc.tensor.transpose(ps[:, B_MISC, k * DH:(k + 1) * DH],
                                               v_t[r:r + DH, k * P:(k + 1) * P],
                                               ident[r:r + DH, r:r + DH])
                last.then_inc(s_vtr, 1)

            def unit_start(it, i):
                if i % 2 == 0:
                    pe.wait_ge(s_wlo, N_AIN + 4 * it + i // 2 + 1)
                if i < 2:
                    if counted(4 * it - 1 + i):
                        pe.wait_ge(s_vz, 4 * it - 1 + i)
                elif i < 6:
                    pe.wait_ge(s_qkraw, 4 * it + i - 1)
                else:
                    pe.wait_ge(s_vz, 4 * it + i - 5)

            def piece(it, i, p):
                if p == 0:
                    unit_start(it, i)
                last = unit_part((N_AIN + i // 2) % 2, B_PROJ + i % 2, i % 2, [p], h_hi, h_lo)
                if p == KT - 1:
                    last.then_inc(s_unit, 1)

            def pieces(it, i, proj, ps_):
                if proj:
                    for p in ps_:
                        piece(it, i, p)

            def iteration(it, proj, att, before):
                for i in range(8):
                    own, at = (it, i - 1) if i else (it - 1, 7)
                    chunks = STEPS[at][1] + 1 if (att and i) or (before and not i) else 0
                    if att:
                        scores(it, i, 0)
                    if proj and i == 7:
                        pe.wait_ge(s_vz, 4 * it + 2)
                        pe.wait_ge(s_qkn, 4 * it + 4)
                    if att and i == 1:
                        pe.wait_ge(s_vlo, 2 * it - 1)
                    pieces(it, i, proj, (0, 1))
                    if proj and i == 7:
                        transpose_v(0)
                    if att and i == 1:
                        transpose_v(1)
                    for c in range(min(2, chunks)):
                        transpose_p(own, at, c)
                    pieces(it, i, proj, (2,))
                    if proj and 2 <= i <= 5:
                        head_square(it, i - 2)
                    pieces(it, i, proj, (3,))
                    if att:
                        scores(it, i, 1)
                    for c in range(4):
                        if c < chunks:
                            pv(own, at, c)
                        if c + 2 < chunks:
                            transpose_p(own, at, c + 2)
                        pieces(it, i, proj, (4 + c,))

            pe.wait_ge(s_msr, 4)
            pe.wait_ge(s_f, 1)
            iteration(0, True, False, False)
            iteration(1, True, True, False)
            with pe.Fori(2, PAIRS) as it:
                iteration(it, True, True, True)
            iteration(PAIRS, False, True, True)
            transpose_p(PAIRS, 7, 0)
            pv(PAIRS, 7, 0)

            pe.wait_ge(s_vz, 4 * PAIRS)
            pe.wait_ge(s_exp, 16 * PAIRS)
            for m in range(KT):
                pe.wait_ge(s_wlo, N_AOUT + m + 1)
                for h in range(2):
                    if counted(2 * m + h - 3):
                        pe.wait_ge(s_or, 2 * m + h - 3)
                    bank = (2 * m + h) % 4
                    unit_part((N_AOUT + m) % 2, bank, h, range(KT - 1), h_hi, h_lo,
                              s_y2l if m == 0 else None, 1, 1)
                    if m == 0:
                        pe.wait_ge(s_y2l, KT + h)
                    unit_part((N_AOUT + m) % 2, bank, h, [KT - 1], h_hi, h_lo).then_inc(s_unit, 1)

        @block.scalar
        def _(act):
            A = nc.scalar.activation

            def split_w(n, slot, turn):
                act.wait_ge(s_wraw[slot], 16 * turn + 16)
                if counted(2 * n - 2):
                    act.wait_ge(s_unit, 2 * n - 2)
                A(w_hi[:, slot, :, :], w_raw[:, slot, :, :], ACT.Copy).then_inc(s_whi, 1)

            act.dma_start(g1[:, :], conv_gain).then_inc(s_const, 16)
            act.dma_start(taps[:, :, :], conv_taps).then_inc(s_const, 16)
            act.dma_start(g2[:, :], attn_gain).then_inc(s_const, 16)
            for side in range(2):
                r = slice(DH * side, DH * side + DH)
                act.dma_start(gq[r, :], q_gain).then_inc(s_const, 16)
                act.dma_start(gk[r, :], k_gain).then_inc(s_const, 16)
            act.dma_start(b_f[:, :], b_forget).then_inc(s_const, 16)

            for c in range(2 * KT):
                h, k = divmod(c, KT)
                if k % 4 == 0:
                    act.wait_ge(s_x[2 * h + k // 4], 16)
                if counted(c - 1):
                    act.wait_ge(s_sqa, c - 1)
                A(sq2[:, (c % 2) * HALF:(c % 2 + 1) * HALF], x_t[:, k, halves(h)], ACT.Square).then_inc(s_sqm, 1)
                if c == 4:
                    split_w(0, 0, 0)

            def rsqrt_guess(turn):
                act.wait_ge(s_msr, 2 * turn + 2)
                A(inv[:, :], mbuf, ACT.Ln).then_inc(s_rs0, 1)
                act.wait_ge(s_rs0, 2 * turn + 1)
                A(inv[:, :], inv[:, :], ACT.Exp, scale=-0.5).then_inc(s_rs0, 1)

            nc.scalar.preload_act_table_set("natural_log_exp_and_others")
            rsqrt_guess(0)

            def conv_block(j):
                for t in range(4):
                    split_w(4 * j + t + 1, (t + 1) % 2, 2 * j + (t + 1) // 2)
                    for h in range(2):
                        if t == 2:
                            act.wait_ge(s_evac, 8 * j + 4 + h + 1)
                            A(gate[:, halves(h)], gate[:, halves(h)], ACT.Silu).then_inc(s_gate, 1)
                        if t == 3:
                            act.wait_ge(s_y, 2 * j + h + 1)
                            A(y_hi[:, j, halves(h)], yb[:, halves(h)], ACT.Copy)\
                                .then_inc(s_yhi, 1)

            conv_block(0)
            with act.Fori(1, KT) as j:
                conv_block(j)

            with act.Fori(0, 2) as i:
                for t in range(4):
                    split_w(N_COUT + 4 * i + t + 1, (t + 1) % 2, 2 * KT + 2 * i + (t + 1) // 2)
                    for h in range(2):
                        u = 8 * i + 2 * t + h
                        act.wait_ge(s_evac, 8 * KT + u + 1)
                        act.wait_ge(s_sqa, 2 * KT + u - 1)
                        A(sq2[:, halves(h)], x_t[:, 4 * i + t, halves(h)], ACT.Square)\
                            .then_inc(s_sqm, 1)

            nc.scalar.preload_act_table_set("natural_log_exp_and_others")
            rsqrt_guess(1)
            split_w(N_AIN, 1, N_AIN // 2)
            f = p_big[0:NH, 0, :]
            act.wait_ge(s_f, 3)
            A(f, f, ACT.Exp).then_inc(s_fa, 1)
            act.wait_ge(s_fa, 1)
            A(f, f, ACT.Ln, bias=1.0).then_inc(s_fa, 1)
            act.wait_ge(s_f, 5)
            A(pt_hi[0:NH, :, :], f.rearrange("p (a n) -> p a n", a=2), ACT.Copy).then_inc(s_fa, 1)
            act.wait_ge(s_fa, 3)
            act.wait_ge(s_f, 6)
            A(v_st[0:NH, 0, :, :], pt_hi[0:NH, :, :].bitcast(F32).rearrange("p a n -> p (a n)"),
              ACT.Copy, scale=-1.0).then_inc(s_fa, 1)
            A(v_st[0:NH, 1, :, :], pt_lo[0:NH, :, :].bitcast(F32).rearrange("p a n -> p (a n)"),
              ACT.Copy, scale=-1.0).then_inc(s_fa, 1)

            def softmax_exp(it, i, par):
                pair = it - 1
                t = STEPS[i][1]
                w = 2 * P * (t + 1)
                col = 2 * (i % 2) + par
                act.wait_ge(s_max, 16 * pair + 2 * i + par + 1)
                if counted(CHUNKS * pair + (CHUNK0[i - 1] if i else 0) - (1 if i == 0 else 0)):
                    act.wait_ge(s_ptr, CHUNKS * pair + (CHUNK0[i - 1] if i else 0) - (1 if i == 0 else 0))
                if counted(16 * pair + 2 * i + par - 3):
                    act.wait_ge(s_rd, 16 * pair + 2 * i + par - 3)
                dst = (p_big if i % 2 == 0 else p_small)[:, par, 0:w]
                if t >= 2:
                    src = ps[:, B_SCORE:B_SCORE + 2, 0:w // 2]
                    dst = dst.rearrange("p (b n) -> p b n", b=2)
                else:
                    src = ps[:, B_SCORE + par, 0:w]
                A(dst, src, ACT.Exp, bias=neg_max[:, col:col + 1],
                  accum_out=denom[:, col:col + 1]).then_inc(s_exp, 1)

            def pt_split(it, g):
                pair = it - 1
                act.wait_ge(s_ptr, CHUNKS * pair + g + 1)
                if counted(CHUNKS * pair + g - 1):
                    act.wait_ge(s_pv, CHUNKS * pair + g - 1)
                A(pt_hi[:, g % 2, :], ps[:, B_PT + g % 2, :], ACT.Copy).then_inc(s_pth, 1)

            def out_copy(it, i):
                pair = it - 1
                side, t = STEPS[i]
                r = DH * side
                act.wait_ge(s_pv, CHUNKS * pair + CHUNK0[i] + t + 1)
                if counted(4 * pair + 2 * side + (0 if t == 2 else 1)):
                    act.wait_ge(s_y2, 4 * pair + 2 * side + (0 if t == 2 else 1))
                A(osum[r:r + DH, :], ps[DH:P, B_OUT, :], ACT.Copy).then_inc(s_oc, 1)

            def stack_q_hi(pair, side):
                own = slice(DH * side, DH * side + DH)
                act.wait_ge(s_qkn, 4 * pair + 2)
                if counted(16 * pair - 8 + 8 * side):
                    act.wait_ge(s_sc, 16 * pair - 8 + 8 * side)
                act.wait_ge(s_clear, 1)
                A(q1[own, side, :], qn[own, :], ACT.Copy)
                A(q2[own, side, :], qn[own, :], ACT.Copy).then_inc(s_qhi, 1)

            def stack_k_hi(pair, side):
                own = slice(DH * side, DH * side + DH)
                other = slice(DH * (1 - side), DH * (1 - side) + DH)
                act.wait_ge(s_qkn, 4 * pair + 4)
                if counted(16 * pair - 8 + 8 * side):
                    act.wait_ge(s_sc, 16 * pair - 8 + 8 * side)
                A(k1[own, side, :], kn[own, :], ACT.Copy)
                A(k1[other, side, :], kn[own, :], ACT.Copy).then_inc(s_khi, 1)

            def v_split(pair, side):
                act.wait_ge(s_vtr, 2 * pair + side + 1)
                if counted(CHUNKS * pair - 10 + 10 * side):
                    act.wait_ge(s_pv, CHUNKS * pair - 10 + 10 * side)
                act.wait_ge(s_cst, 64)
                A(v_st[:, side, :, 0:DH], ps[:, B_MISC, :].rearrange("p (k d) -> p k d", d=DH),
                  ACT.Copy).then_inc(s_vhi, 1)

            def iteration(it, proj, att, before):
                for i in range(8):
                    own, at = (it, i - 1) if i else (it - 1, 7)
                    chunks = STEPS[at][1] + 1 if (att and i) or (before and not i) else 0
                    if proj and i % 2 == 0:
                        n = N_AIN + 4 * it + i // 2 + 1
                        split_w(n, (N_AIN + i // 2 + 1) % 2, 2 * it + (N_AIN + i // 2 + 1) // 2)
                    if att:
                        softmax_exp(it, i, 0)
                    for c in range(min(2, chunks)):
                        pt_split(own, CHUNK0[at] + c)
                    if att and i == 0:
                        z_exp(it - 1, 1)
                        stack_q_hi(it - 1, 1)
                    if att and i == 1:
                        v_split(it - 1, 1)
                        stack_k_hi(it - 1, 1)
                    if proj and 2 <= i <= 5:
                        guess(it, i - 2)
                    if proj and i == 6:
                        stack_q_hi(it, 0)
                    if proj and i == 7:
                        v_split(it, 0)
                    if att:
                        softmax_exp(it, i, 1)
                    for c in range(2, chunks):
                        pt_split(own, CHUNK0[at] + c)
                    if proj and 1 <= i <= 4:
                        square(it, i - 1)
                    if proj and i == 6:
                        stack_k_hi(it, 0)
                    if proj and i == 7:
                        z_exp(it, 0)
                    if att and not proj and i:
                        y2_split(i - 1, None)
                    if chunks and STEPS[at][1] % 2 == 0:
                        out_copy(own, at)

            def guess(it, u):
                act.wait_ge(s_ssq, 4 * it + u + 1)
                if counted(4 * it + u):
                    act.wait_ge(s_qkn, 4 * it + u)
                A(y0, ps[:, B_MISC, :], ACT.Ln, bias=eps_col[:, :]).then_inc(s_guess, 1)
                act.wait_ge(s_guess, 8 * it + 2 * u + 1)
                A(y0, y0, ACT.Exp, scale=-0.5).then_inc(s_guess, 1)

            def square(it, u):
                act.wait_ge(s_qkraw, 4 * it + u + 1)
                if counted(4 * it + u):
                    act.wait_ge(s_ssq, 4 * it + u)
                if u == 0:
                    if counted(4 * it):
                        act.wait_ge(s_gz, 4 * it)
                A(sq, (qn, kn)[u // 2][:, halves(u % 2)], ACT.Square).then_inc(s_qsq, 1)

            def z_exp(it, h):
                act.wait_ge(s_vz, 4 * it + 3 + h)
                if h:
                    act.wait_ge(s_gz, 4 * it + 2)
                else:
                    act.wait_ge(s_ssq, 4 * it + 4)
                A(sq, y2[:, it, halves(h)], ACT.Exp, scale=-1.0).then_inc(s_ze, 1)

            def y2_split(k, h):
                cols = slice(0, S) if h is None else halves(h)
                act.wait_ge(s_unit, 2 * N_AOUT)
                act.wait_ge(s_y2, 4 * k + 4)
                A(h_hi[:, k, cols], y2[:, k, cols], ACT.Copy).then_inc(s_y2h, 1)

            iteration(0, True, False, False)
            iteration(1, True, True, False)
            with act.Fori(2, PAIRS) as it:
                iteration(it, True, True, True)
            iteration(PAIRS, False, True, True)
            pt_split(PAIRS, CHUNK0[7])
            out_copy(PAIRS, 7)
            y2_split(KT - 1, 0)
            y2_split(KT - 1, 1)

            for m in range(KT):
                if m + 1 < KT:
                    n = N_AOUT + m + 1
                    split_w(n, n % 2, n // 2)
        @block.vector
        def _(dve):
            v = nc.vector
            TT, TS, STT = v.tensor_tensor, v.tensor_scalar, v.scalar_tensor_tensor
            steps = [0]

            def own(ins):
                steps[0] += 1
                ins.then_inc(s_dve, 1)
                dve.wait_ge(s_dve, steps[0])

            v.memset(mean_d[:, :], 1.0 / D)
            v.memset(eps_col[:, :], EPS)
            for a in range(2):
                for b in range(2):
                    v.memset(mean_h[a * DH:(a + 1) * DH, b * DH:(b + 1) * DH], 1.0 / DH if a == b else 0.0)
            v.memset(mask_bf[:, 0:P], 0.0)
            v.memset(mask_bf[:, P:2 * P], MASKED).then_inc(s_vconst, 1)
            dve.wait_ge(s_const, 16 * 8)
            own(TS(gq[:, :], gq[:, :], -0.5 / DH ** 0.5, None, ALU.mult))
            own(TS(gk[:, :], gk[:, :], -0.5, None, ALU.mult))
            for c in range(2 * KT):
                h, k = divmod(c, KT)
                if k % 4 == 0:
                    dve.wait_ge(s_x[2 * h + k // 4], 16)
                own(TS(h_hi[:, k, halves(h)], x_t[:, k, halves(h)], g1[:, k:k + 1], None, ALU.mult))
                STT(h_lo[:, k, halves(h)], x_t[:, k, halves(h)], g1[:, k:k + 1],
                    h_hi[:, k, halves(h)].bitcast(F32), ALU.mult, ALU.subtract).then_inc(s_h, 1)

            def rsqrt(turn, banks):
                for h in range(2):
                    dve.wait_ge(s_ms, 2 * turn + h + 1)
                    TS(mbuf[:, halves(h)], ps[:, banks + h, :], EPS, None, ALU.add).then_inc(s_msr, 1)
                dve.wait_ge(s_rs0, 2 * turn + 2)
                t = ubuf[:, 0:S]
                own(TT(t, inv[:, :], inv[:, :], ALU.mult))
                own(STT(t, t, -0.5, mbuf, ALU.mult, ALU.mult))
                own(STT(inv[:, :], t, 1.5, inv[:, :], ALU.add, ALU.mult))
                return v.memset(ubuf[:, 0:2], 0.0).then_inc(s_inv, 1)

            rsqrt(0, 4)
            dve.wait_ge(s_inv, 1)

            with dve.Fori(0, KT) as j:
                base = steps[0] + j * 8
                local = 0
                for t in range(4):
                    for h in range(2):
                        u = 2 * t + h
                        hs = halves(h)
                        dve.wait_ge(s_unit, 8 * j + u + 1)
                        if t == 0:
                            TT(ca[:, hs], ps[:, u, :], inv[:, hs], ALU.mult).then_inc(s_evac, 1)
                        if t == 1:
                            dve.wait_ge(s_evac, 8 * j + h + 1)
                            TT(ubuf[:, 2 + h * HALF:2 + (h + 1) * HALF], ps[:, u, :], ca[:, hs],
                               ALU.mult).then_inc(s_evac, 1)
                            dve.wait_ge(s_u, 2 * j + h + 1)
                            for i in range(TAPS):
                                w = taps[:, TAPS - 1 - i, bass.ds(j, 1)]
                                us = ubuf[:, 2 + h * HALF - i:2 + (h + 1) * HALF - i]
                                if i == 0:
                                    ins = TS(ca[:, hs], us, w, None, ALU.mult)
                                else:
                                    ins = STT(ca[:, hs], us, w, ca[:, hs], ALU.mult, ALU.add)
                                local += 1
                                ins.then_inc(s_dve, 1)
                                dve.wait_ge(s_dve, base + local)
                        if t == 2:
                            TT(gate[:, hs], ps[:, u, :], inv[:, hs], ALU.mult).then_inc(s_evac, 1)
                        if t == 3:
                            TT(yb[:, hs], ps[:, u, :], inv[:, hs], ALU.mult).then_inc(s_evac, 1)
                            dve.wait_ge(s_evac, 8 * j + u + 1)
                            local += 1
                            TT(yb[:, hs], yb[:, hs], ca[:, hs], ALU.mult).then_inc(s_dve, 1)
                            dve.wait_ge(s_dve, base + local)
                            dve.wait_ge(s_gate, 2 * j + h + 1)
                            TT(yb[:, hs], yb[:, hs], gate[:, hs], ALU.mult).then_inc(s_y, 1)
                            dve.wait_ge(s_yhi, 2 * j + h + 1)
                            TT(y_lo[:, j, hs], yb[:, hs],
                               y_hi[:, j, hs].bitcast(F32), ALU.subtract).then_inc(s_ylo, 1)
                assert local == 8
            steps[0] += 8 * KT

            with dve.Fori(0, 2) as i:
                base = steps[0] + i * 8
                for t in range(4):
                    for h in range(2):
                        u = 2 * t + h
                        hs = halves(h)
                        m = 4 * i + t
                        gain = g2[:, bass.ds(m, 1)]
                        dve.wait_ge(s_unit, 8 * KT + 8 * i + u + 1)
                        TT(x_t[:, m, hs], ps[:, u, :], x_t[:, m, hs], ALU.add).then_inc(s_evac, 1)
                        dve.wait_ge(s_evac, 8 * KT + 8 * i + u + 1)
                        TS(h_hi[:, m, hs], x_t[:, m, hs], gain, None, ALU.mult).then_inc(s_dve, 1)
                        dve.wait_ge(s_dve, base + u + 1)
                        STT(h_lo[:, m, hs], x_t[:, m, hs], gain, h_hi[:, m, hs].bitcast(F32),
                            ALU.mult, ALU.subtract).then_inc(s_h, 1)
            steps[0] += 16

            rsqrt(1, 2)
            dve.wait_ge(s_inv, 2)
            dve.wait_ge(s_spill, 16 * KT)
            f, m0, ones = p_big[0:NH, 0, :], p_big[0:NH, 1, :], kn[0:NH, :]
            v.memset(ones, 1.0)
            for h in range(2):
                dve.wait_ge(s_unit, 2 * N_FORGET + h + 1)
                ins = TT(f[:, halves(h)], ps[0:NH, h, :], inv[0:NH, halves(h)], ALU.mult)
            ins.then_inc(s_f, 1)
            dve.wait_ge(s_f, 1)
            own(TS(f, f, b_f[:, :], None, ALU.add))
            TS(m0, f, 0.0, None, ALU.min).then_inc(s_f, 1)
            dve.wait_ge(s_f, 2)
            STT(f, m0, 2.0, f, ALU.mult, ALU.subtract).then_inc(s_f, 1)
            dve.wait_ge(s_fa, 2)
            TT(m0, m0, f, ALU.subtract).then_inc(s_f, 1)
            dve.wait_ge(s_f, 4)
            v.tensor_tensor_scan(f, ones, m0, 0.0, ALU.mult, ALU.add).then_inc(s_f, 1)
            dve.wait_ge(s_fa, 3)
            TT(pt_lo[0:NH, :, :].rearrange("p a n -> p (a n)"), f,
               pt_hi[0:NH, :, :].bitcast(F32).rearrange("p a n -> p (a n)"), ALU.subtract).then_inc(s_f, 1)

            def row_max(it, i, par):
                pair = it - 1
                t = STEPS[i][1]
                w = 2 * P * (t + 1)
                col = 2 * (i % 2) + par
                dve.wait_ge(s_sc, 16 * pair + 2 * i + par + 1)
                if t >= 2:
                    src, ax = ps[:, B_SCORE:B_SCORE + 2, 0:w // 2], AX.XY
                else:
                    src, ax = ps[:, B_SCORE + par, 0:w], AX.X
                v.tensor_reduce(neg_max[:, col:col + 1], src, ax, ALU.max, negate=True).then_inc(s_max, 1)

            def invert(it, i, par):
                pair = it - 1
                col = 2 * (i % 2) + par
                dve.wait_ge(s_exp, 16 * pair + 2 * i + par + 1)
                if counted(16 * pair + 2 * i + par - 3):
                    dve.wait_ge(s_pn, 16 * pair + 2 * i + par - 3)
                v.reciprocal(rdenom[:, col:col + 1], denom[:, col:col + 1]).then_inc(s_rd, 1)

            def pt_low(it, g):
                pair = it - 1
                dve.wait_ge(s_pth, CHUNKS * pair + g + 1)
                TT(pt_lo[:, g % 2, :], ps[:, B_PT + g % 2, :], pt_hi[:, g % 2, :].bitcast(F32),
                   ALU.subtract).then_inc(s_ptl, 1)

            def out_sum(it, i):
                side, t = STEPS[i]
                r = DH * side
                dve.wait_ge(s_oc, 4 * (it - 1) + 2 * side + (1 if t == 2 else 2))
                TT(osum[r:r + DH, :], ps[0:DH, B_OUT, :], osum[r:r + DH, :], ALU.add).then_inc(s_os, 1)

            def out_gate(it, i):
                pair = it - 1
                side, t = STEPS[i]
                r = DH * side
                dve.wait_ge(s_os, 4 * pair + 2 * side + (1 if t == 2 else 2))
                dve.wait_ge(s_gz, 4 * pair + 4)
                dst = y2[r:r + DH, pair, halves(1 if t == 2 else 0)]
                TT(dst, osum[r:r + DH, :], dst, ALU.mult).then_inc(s_y2, 1)

            def stack_q_lo(pair, side):
                o, r = DH * side, DH * (1 - side)
                dve.wait_ge(s_qhi, 2 * pair + side + 1)
                TT(q1[r:r + DH, side, :], qn[o:o + DH, :], q1[o:o + DH, side, :].bitcast(F32),
                   ALU.subtract).then_inc(s_stq, 1)

            def v_low(pair, side):
                dve.wait_ge(s_vhi, 2 * pair + side + 1)
                TT(v_st[:, side, :, DH:P], ps[:, B_MISC, :].rearrange("p (k d) -> p k d", d=DH),
                   v_st[:, side, :, 0:DH].bitcast(F32), ALU.subtract).then_inc(s_vlo, 1)

            NEWTON = 3

            def refine(it, u, base, local):
                dst = (qn, kn)[u // 2][:, halves(u % 2)]
                dve.wait_ge(s_guess, 8 * it + 2 * u + 2)
                if counted(2 * it):
                    dve.wait_ge(s_vtr, 2 * it)
                TT(newton, y0, y0, ALU.mult).then_inc(s_dve, 1)
                dve.wait_ge(s_dve, base + local + 1)
                STT(newton, ps[:, B_MISC, :], EPS, newton, ALU.add, ALU.mult).then_inc(s_dve, 1)
                dve.wait_ge(s_dve, base + local + 2)
                STT(newton, newton, 3.0, y0, ALU.subtract, ALU.mult).then_inc(s_dve, 1)
                dve.wait_ge(s_dve, base + local + 3)
                STT(dst, dst, (gq, gk)[u // 2][:, :], newton, ALU.mult, ALU.mult).then_inc(s_qkn, 1)
                return local + NEWTON

            def qk_evac(it, u):
                dve.wait_ge(s_unit, 2 * N_AIN + 8 * it + u + 1)
                if u < 2:
                    if counted(2 * it):
                        dve.wait_ge(s_stq, 2 * it)
                else:
                    if counted(2 * it):
                        dve.wait_ge(s_khi, 2 * it)
                        dve.wait_ge(s_stk, 2 * it)
                TT((qn, kn)[u // 2][:, halves(u % 2)], ps[:, B_PROJ + u % 2, :],
                   inv[:, halves(u % 2)], ALU.mult).then_inc(s_qkraw, 1)

            def vz_evac(it, u):
                h = u % 2
                dve.wait_ge(s_unit, 2 * N_AIN + 8 * it + u + 1)
                if u < 6:
                    if counted(2 * it):
                        dve.wait_ge(s_vtr, 2 * it)
                    if u == 5:
                        dve.wait_ge(s_qkn, 4 * it + 4)
                    dst = v_t[:, halves(h)]
                else:
                    dst = y2[:, it, halves(h)]
                TT(dst, ps[:, B_PROJ + h, :], inv[:, halves(h)], ALU.mult).then_inc(s_vz, 1)

            def z_gate(it, h, part, base, local):
                quarter = slice(part * HALF // 2, (part + 1) * HALF // 2)
                e = sq[:, quarter]
                dve.wait_ge(s_ze, 2 * it + h + 1)
                TS(e, e, 1.0, None, ALU.add).then_inc(s_dve, 1)
                dve.wait_ge(s_dve, base + local + 1)
                v.reciprocal(e, e).then_inc(s_dve, 1)
                dve.wait_ge(s_dve, base + local + 2)
                dst = y2[:, it, halves(h)][:, quarter]
                TT(dst, dst, e, ALU.mult).then_inc(s_gz, 1)
                return local + 2

            def iteration(it, proj, att, before, base):
                local = 0
                for i in range(8):
                    own, at = (it, i - 1) if i else (it - 1, 7)
                    chunks = STEPS[at][1] + 1 if (att and i) or (before and not i) else 0
                    if att:
                        row_max(it, i, 0)
                    if att and i and STEPS[i - 1][1] in (1, 3) and (i >= 2 or before):
                        out_gate(*((it, i - 2) if i >= 2 else (it - 1, 7)))
                    if att and i == 0:
                        vz_evac(it - 1, 7)
                    if proj and 1 <= i <= 4:
                        qk_evac(it, i - 1)
                    if proj and 5 <= i:
                        vz_evac(it, i - 1)
                    if att:
                        invert(it, i, 0)
                    for c in range(min(2, chunks)):
                        pt_low(own, CHUNK0[at] + c)
                    if att and i == 0:
                        local = z_gate(it - 1, 1, 0, base, local)
                    if att:
                        row_max(it, i, 1)
                    if att and i == 0:
                        stack_q_lo(it - 1, 1)
                        local = z_gate(it - 1, 1, 1, base, local)
                    if att and i == 1:
                        v_low(it - 1, 1)
                    if proj and i == 7:
                        v_low(it, 0)
                    for c in range(2, chunks):
                        pt_low(own, CHUNK0[at] + c)
                    if att:
                        invert(it, i, 1)
                    if proj and 2 <= i <= 5:
                        local = refine(it, i - 2, base, local)
                    if proj and i == 6:
                        stack_q_lo(it, 0)
                    if proj and i == 7:
                        local = z_gate(it, 0, 0, base, local)
                        local = z_gate(it, 0, 1, base, local)
                    if chunks and STEPS[at][1] % 2 == 0:
                        out_sum(own, at)
                return local

            for side in range(2):
                r = DH * (1 - side)
                for st in (q2, k2):
                    own(v.memset(st[r:r + DH, side, :].bitcast(F32), 0.0))
            for side in range(2):
                r = DH * (1 - side)
                for st in (q2, k2):
                    ins = v.memset(st[r:r + 4, side, :].bitcast(F32), 1.0)
            ins.then_inc(s_clear, 1)
            dve.wait_ge(s_cst, 64)
            first = steps[0] + iteration(0, True, False, False, steps[0])
            per = iteration(1, True, True, False, first)
            with dve.Fori(2, PAIRS) as it:
                iteration(it, True, True, True, first + (it - 1) * per)
            iteration(PAIRS, False, True, True, first + (PAIRS - 1) * per)
            pt_low(PAIRS, CHUNK0[7])
            out_sum(PAIRS, 7)
            out_gate(PAIRS, 7)

            for m in range(KT):
                for h in range(2):
                    dve.wait_ge(s_unit, 2 * (N_AOUT + m) + h + 1)
                    dve.wait_ge(s_x1r[m % 2], 16 * (m // 2 + 1))
                    if counted(16 * (m // 2)):
                        dve.wait_ge(s_out[2 * (m % 2) + h], 16 * (m // 2))
                    TT(p_big[:, m % 2, halves(h)], ps[:, (2 * m + h) % 4, :],
                       (qn, kn)[m % 2][:, halves(h)], ALU.add).then_inc(s_or, 1)

        @block.gpsimd
        def _(pool):
            g = nc.gpsimd
            TT = g.tensor_tensor
            g.memset(ident[:, :], 0.0).then_inc(s_ident, 1)
            pool.wait_ge(s_ident, 1)
            g.affine_select(out=ident[:, :], in_=ident[:, :], compare_op=ALU.not_equal, fill=1.0, base=0,
                            pattern=[[-1, P]], channel_multiplier=1).then_inc(s_ident, 1)
            g.memset(acc, 0.0).then_inc(s_zero, 1)
            pool.wait_ge(s_zero, 1)
            pool.wait_ge(s_vconst, 1)
            pool.wait_ge(s_ident, 2)
            g.affine_select(out=mask_bf[:, 0:P], in_=mask_bf[:, 0:P], compare_op=ALU.is_ge, fill=MASKED,
                            base=0, pattern=[[-1, P]], channel_multiplier=1)
            g.tensor_copy(ident_bf[:, :], ident[:, :]).then_inc(s_ident, 1)

            def w_low(n, slot):
                pool.wait_ge(s_whi, n + 1)
                TT(w_lo[:, slot, :, :], w_raw[:, slot, :, :], w_hi[:, slot, :, :].bitcast(F32),
                   ALU.subtract).then_inc(s_wlo, 1)

            def add_square(k, c, h):
                pool.wait_ge(s_sqm, c + 1)
                if counted(c):
                    pool.wait_ge(s_sqa, c)
                TT(acc[:, halves(h)], acc[:, halves(h)], sq2[:, (c % 2) * HALF:(c % 2 + 1) * HALF],
                   ALU.add).then_inc(s_sqa, 1)

            for c in range(2 * KT):
                add_square(c % KT, c, c // KT)
                if c == 3:
                    w_low(0, 0)

            with pool.Fori(0, KT) as j:
                for t in range(4):
                    w_low(4 * j + t + 1, (t + 1) % 2)
                    if t == 1:
                        for h in range(2):
                            pool.wait_ge(s_evac, 8 * j + 2 + h + 1)
                            pool.wait_ge(s_inv, 1)
                            us = ubuf[:, 2 + h * HALF:2 + (h + 1) * HALF]
                            TT(us, us, inv[:, halves(h)], ALU.mult).then_inc(s_u, 1)

            pool.wait_ge(s_ylo, 2 * KT)
            g.memset(acc, 0.0).then_inc(s_zero, 1)
            pool.wait_ge(s_zero, 2)
            with pool.Fori(0, 2) as i:
                for t in range(4):
                    w_low(N_COUT + 4 * i + t + 1, (t + 1) % 2)
                    for h in range(2):
                        c = 2 * KT + 8 * i + 2 * t + h
                        pool.wait_ge(s_sqm, c + 1)
                        pool.wait_ge(s_sqa, c)
                        TT(acc[:, halves(h)], acc[:, halves(h)], sq2[:, halves(h)], ALU.add)\
                            .then_inc(s_sqa, 1)
            w_low(N_AIN, 1)

            def normalise(it, i, par):
                pair = it - 1
                w = 2 * P * (STEPS[i][1] + 1)
                col = 2 * (i % 2) + par
                pool.wait_ge(s_rd, 16 * pair + 2 * i + par + 1)
                p = (p_big if i % 2 == 0 else p_small)[:, par, 0:w]
                TT(p, p, rdenom[:, col:col + 1].broadcast_to([P, w]), ALU.mult).then_inc(s_pn, 1)

            def stack_k_lo(pair, side):
                r = DH * side
                pool.wait_ge(s_khi, 2 * pair + side + 1)
                TT(k2[r:r + DH, side, :], kn[r:r + DH, :], k1[r:r + DH, side, :].bitcast(F32),
                   ALU.subtract).then_inc(s_stk, 1)
                pool.wait_ge(s_stk, 2 * pair + side + 1)

            def y2_low(k, cols):
                pool.wait_ge(s_y2h, k)
                TT(h_lo[:, min(k - 1, KT - 1), cols], y2[:, min(k - 1, KT - 1), cols],
                   h_hi[:, min(k - 1, KT - 1), cols].bitcast(F32), ALU.subtract).then_inc(s_y2l, 1)

            def iteration(it, proj, att):
                for i in range(8):
                    if proj and i % 2 == 0:
                        w_low(N_AIN + 4 * it + i // 2 + 1, (N_AIN + i // 2 + 1) % 2)
                    if att:
                        normalise(it, i, 0)
                    if att and i == 1:
                        pool.wait_ge(s_pn, 16 * it - 13)
                        stack_k_lo(it - 1, 1)
                    if proj and i == 7:
                        if att:
                            pool.wait_ge(s_pn, 16 * it - 1)
                        else:
                            pool.wait_ge(s_wlo, N_AIN + 4 * it + 5)
                        stack_k_lo(it, 0)
                    if att:
                        normalise(it, i, 1)
                    if att and not proj and i:
                        y2_low(i, slice(0, S))

            iteration(0, True, False)
            iteration(1, True, True)
            with pool.Fori(2, PAIRS) as it:
                iteration(it, True, True)
            iteration(PAIRS, False, True)
            y2_low(KT, halves(0))
            y2_low(KT + 1, halves(1))
            for m in range(KT - 1):
                w_low(N_AOUT + m + 1, (N_AOUT + m + 1) % 2)


def kernel(**inputs):
    import numpy as np
    import concourse.bacc as bacc
    from concourse.bass_utils import run_bass_kernel_spmd

    nc = bacc.Bacc("TRN2", target_bir_lowering=False, num_devices=1)

    def tiles(w, blocks, order):
        w = w.reshape(KT, P, blocks, KT, P).transpose(3, 2, 1, 0, 4)[:, order]
        return w.reshape(KT * blocks, P, KT, P)

    def rows(v):
        return np.moveaxis(v.reshape(*v.shape[:-1], KT, P), -1, 0)

    w_a = inputs["attn_w_in"][0]
    laid_out = {
        "x": inputs["x"][0].T.reshape(KT, P, S).transpose(1, 0, 2),
        "w_cin": tiles(inputs["conv_w_in"][0], 4, CONV_COLUMNS),
        "w_cout": tiles(inputs["conv_w_out"][0], 1, [0]),
        "w_ain": tiles(w_a[:, :4 * D], 4, [0, 1, 2, 3]),
        "w_forget": w_a[:, 4 * D:].reshape(KT, P, NH).transpose(1, 0, 2),
        "w_aout": tiles(inputs["attn_w_out"][0], 1, [0]),
        "conv_gain": rows(inputs["conv_norm_g"][0]),
        "conv_taps": rows(inputs["conv_w"][0]),
        "attn_gain": rows(inputs["attn_norm_g"][0]),
        "b_forget": inputs["attn_b_f"][0].reshape(NH, 1),
        "q_gain": inputs["attn_q_norm_g"][0].reshape(DH, 1),
        "k_gain": inputs["attn_k_norm_g"][0].reshape(DH, 1),
    }
    arrays, args = {}, []
    for name, a in laid_out.items():
        a = np.ascontiguousarray(a)
        arrays[f"in_{name}"] = a
        args.append(nc.dram_tensor(f"in_{name}", a.shape, mybir.dt.from_np(a.dtype), kind="ExternalInput").ap())
    args.append(nc.dram_tensor("out", (P, KT, S), F32, kind="ExternalOutput").ap())
    hybrid(nc, *args)
    result = run_bass_kernel_spmd(nc, [arrays], core_ids=[0])
    return result.results[0]["out"].transpose(2, 1, 0).reshape(1, S, D)
```

```python
import concourse.bass as bass
from concourse import mybir
from contextlib import ExitStack

F32 = mybir.dt.float32
F32R = mybir.dt.float32r
BF16 = mybir.dt.bfloat16
ALU = mybir.AluOpType
ACT = mybir.ActivationFunctionType
AX = mybir.AxisListType

P = 128
D = 1024
S = 1024
KT = D // P
NH = 16
DH = D // NH
PAIRS = NH // 2
HALF = S // 2
TAPS = 3
EPS = 1e-6
MASKED = -3.0e38

N_CIN, N_COUT, N_FORGET, N_AIN, N_AOUT = 0, 4 * KT, 5 * KT, 5 * KT + 1, 9 * KT + 1
N_TILES = 10 * KT + 1
CONV_COLUMNS = [1, 2, 3, 0]
ATTN_COLUMNS = [0, 1, 3, 2]
B_PROJ, B_SCORE, B_PT, B_OUT, B_MISC = 0, 2, 4, 6, 7
STEPS = [(x, t) for x in range(2) for t in (3, 2, 1, 0)]
CHUNK0 = [0, 4, 7, 9, 10, 14, 17, 19]
CHUNKS = 20
AHEAD = 4


def counted(value):
    return not isinstance(value, int) or value > 0


def hybrid(nc, x, w_cin, w_cout, w_ain, w_forget, w_aout, conv_gain, conv_taps, attn_gain, b_forget,
           q_gain, k_gain, out):
    x1_dram = nc.dram_tensor("x1_dram", [P, KT, S], F32, kind="Internal").ap()
    c_dram = nc.dram_tensor("c_dram", [NH, 4, S], F32, kind="Internal").ap()

    with ExitStack() as ctx:
        def sb(name, shape, dt=F32, where=ctx):
            return where.enter_context(nc.sbuf_tensor(name, shape, dt))

        def sem(name):
            return ctx.enter_context(nc.semaphore(name))

        ps = ctx.enter_context(nc.psum_tensor("ps", [P, 8, HALF], F32))

        h_hi = sb("h_hi", [P, KT, S], F32R)
        h_lo = sb("h_lo", [P, KT, S], F32R)
        w_raw = sb("w_raw", [P, 2, KT, P])
        w_hi = sb("w_hi", [P, 2, KT, P], F32R)
        w_lo = sb("w_lo", [P, 2, KT, P], F32R)
        inv_ctx = ExitStack()
        inv = sb("inv", [P, S], where=inv_ctx)
        inv_ctx.close()
        w7_hi = sb("w7_hi", [P, AHEAD, P], F32R)
        w7_lo = sb("w7_lo", [P, AHEAD, P], F32R)
        scr_ctx = ExitStack()
        scr = sb("scr", [P, 3 * S], where=scr_ctx)
        ubuf = sb("ubuf", [P, S + 8], where=scr_ctx)
        scr_ctx.close()
        sq_hi = sb("sq_hi", [P, HALF], F32R)
        y0 = sb("y0", [P, HALF])
        osum = sb("osum", [P, HALF])
        p_small = sb("p_small", [P, 2, 3 * P * 2])
        v_ctx = ExitStack()
        v_t = sb("v_t", [P, S], where=v_ctx)
        v_ctx.close()
        sq_ctx = ExitStack()
        sq_raw = sb("sq_raw", [P, HALF], where=sq_ctx)
        sq_ctx.close()
        sq_lo = sb("sq_lo", [P, HALF], F32R)
        newton = sb("newton", [P, HALF])
        sb("ubuf_end", [P, 8])
        ident = sb("ident", [P, P])
        ident_bf = sb("ident_bf", [P, P], BF16)
        mask_bf = sb("mask_bf", [P, 2 * P], BF16)
        mean_d = sb("mean_d", [P, P])
        mean_h = sb("mean_h", [P, P], F32R)
        g1 = sb("g1", [P, KT])
        g2 = sb("g2", [P, KT])
        taps = sb("taps", [P, TAPS, KT])
        gq = sb("gq", [P, 1])
        gk = sb("gk", [P, 1])
        b_f = sb("b_f", [NH, 1])
        eps_col = sb("eps_col", [P, 1])
        neg_max = sb("neg_max", [P, 4])
        denom = sb("denom", [P, 4])
        rdenom = sb("rdenom", [P, 4])

        acc = scr[:, 0:S]
        sq2 = scr[:, S:2 * S]
        mbuf = scr[:, 2 * S:3 * S]
        ca = scr[:, 0:S]
        gate = scr[:, S:2 * S]
        yb = scr[:, 2 * S:3 * S]

        conv_ctx = ExitStack()
        x_t = sb("x_t", [P, KT, S], where=conv_ctx)
        y_hi = sb("y_hi", [P, KT, S], F32R, where=conv_ctx)
        y_lo = sb("y_lo", [P, KT, S], F32R, where=conv_ctx)
        conv_ctx.close()

        y2 = sb("y2", [P, KT, S])
        q1 = sb("q1", [P, 2, S], F32R)
        k1 = sb("k1", [P, 2, S], F32R)
        q2 = sb("q2", [P, 2, S], F32R)
        k2 = sb("k2", [P, 2, S], F32R)
        qn = sb("qn", [P, S])
        kn = sb("kn", [P, S])
        v_st = sb("v_st", [P, 2, KT, P], F32R)
        p_big = sb("p_big", [P, 2, S])
        pt_hi = sb("pt_hi", [P, 2, HALF], F32R)
        pt_lo = sb("pt_lo", [P, 2, HALF], F32R)

        s_const = sem("const_landed")
        s_ident = sem("identity_made")
        s_vconst = sem("constants_made")
        s_g1 = sem("conv_gain_landed")
        s_x = [sem(f"x_landed{i}") for i in range(KT)]
        s_hh = sem("h_hi_made")
        s_wraw = [sem(f"w_landed{i}") for i in range(2)]
        s_whi = sem("w_hi_made")
        s_wlo = sem("w_lo_made")
        s_unit = sem("units_done")
        s_sqm = sem("squares_made")
        s_sqa = sem("squares_added")
        s_sq1 = sem("squares_of_half_1_added")
        s_h = sem("h_ready")
        s_ms = sem("mean_square_done")
        s_msr = sem("mean_square_read")
        s_rs0 = sem("rsqrt_guessed")
        s_inv = sem("inv_ready")
        s_evac = sem("conv_units_evacuated")
        s_u = sem("u_scaled")
        s_gate = sem("gate_made")
        s_y = sem("y_made")
        s_yhi = sem("y_hi_made")
        s_ylo = sem("y_lo_made")
        s_spill = sem("x1_stored")
        s_clear = sem("stacks_cleared")
        s_f = sem("forget_steps")
        s_fa = sem("forget_act_steps")
        s_cst = sem("c_stored")
        s_crow = [sem(f"c_rows_landed{i}") for i in range(2)]
        s_qkraw = sem("qk_evacuated")
        s_vz = sem("vz_evacuated")
        s_qsq = sem("qk_squared")
        s_sqp = sem("squares_made_by_gpsimd")
        s_sql = sem("squares_lo_made")
        s_ssq = sem("head_square_done")
        s_guess = sem("head_rsqrt_guessed")
        s_qkn = sem("qk_normed")
        s_qhi = sem("stack_q_hi_made")
        s_khi = sem("stack_k_hi_made")
        s_stq = sem("stack_q_lo_made")
        s_stk = sem("stack_k_lo_made")
        s_vtr = sem("v_transposed")
        s_vhi = sem("v_hi_made")
        s_vlo = sem("v_lo_made")
        s_sc = sem("scores_done")
        s_max = sem("row_max_done")
        s_exp = sem("exp_done")
        s_rd = sem("denominators_inverted")
        s_pn = sem("p_normalised")
        s_ptr = sem("p_transposed")
        s_pth = sem("pt_hi_made")
        s_ptl = sem("pt_lo_made")
        s_pv = sem("pv_done")
        s_oc = sem("out_lo_half_copied")
        s_os = sem("out_halves_summed")
        s_y2 = sem("y2_made")
        s_gz = sem("z_gate_made")
        s_y2h = sem("y2_hi_made")
        s_y2l = sem("y2_lo_made_by_gpsimd")
        s_y2v = sem("y2_lo_made_by_vector")
        s_w7 = sem("w7_copied")
        s_pre = sem("out_ahead_added")
        s_tail = sem("out_tail_done")
        s_fin = sem("out_tail_added")
        s_x1r = [sem(f"x1_reloaded{i}") for i in range(2)]
        s_or = sem("out_residual_added")
        s_out = sem("out_stored")
        s_dve = sem("vector_steps")
        s_zero = sem("sums_cleared")

        block = ctx.enter_context(nc.Block())

        def halves(h):
            return slice(h * HALF, (h + 1) * HALF)

        @block.sync
        def _(sp):
            def load_w(src, n, slot, tile):
                if counted(n - 1):
                    sp.wait_ge(s_whi, n - 1)
                    sp.wait_ge(s_wlo, n - 1)
                sp.dma_start(w_raw[:, slot, :, :], src[tile]).then_inc(s_wraw[slot], 16)

            def load_x(i):
                h, ks = i // 4, slice(2 * (i % 4), 2 * (i % 4) + 2)
                sp.dma_start(x_t[:, ks, halves(h)], x[:, ks, halves(h)]).then_inc(s_x[i], 16)

            load_w(w_cin, 0, 0, 0)
            for i in range(4):
                load_x(i)
            load_w(w_cin, 1, 1, 1)
            for i in range(4, 8):
                load_x(i)
            sp.dma_start(taps[:, :, :], conv_taps).then_inc(s_const, 16)
            sp.dma_start(g2[:, :], attn_gain).then_inc(s_const, 16)
            for side in range(2):
                r = slice(DH * side, DH * side + DH)
                sp.dma_start(gq[r, :], q_gain).then_inc(s_const, 16)
                sp.dma_start(gk[r, :], k_gain).then_inc(s_const, 16)
            sp.dma_start(b_f[:, :], b_forget).then_inc(s_const, 16)
            load_w(w_cin, 2, 0, 2)
            load_w(w_cin, 3, 1, 3)
            with sp.Fori(1, KT) as j:
                for t in range(4):
                    load_w(w_cin, 4 * j + t, t % 2, 4 * j + t)
            for m in range(KT + 3):
                if m < KT:
                    load_w(w_cout, N_COUT + m, m % 2, m)
                elif m == KT:
                    sp.wait_ge(s_whi, N_FORGET - 1)
                    sp.wait_ge(s_wlo, N_FORGET - 1)
                    sp.dma_start(w_raw[:, 0, :, 0:NH], w_forget).then_inc(s_wraw[0], 16)
                else:
                    load_w(w_ain, N_AIN + m - KT - 1, m % 2, m - KT - 1)
                if m >= 3:
                    sp.wait_ge(s_evac, 8 * KT + 2 * (m - 3) + 2)
                    sp.dma_start(x1_dram[:, m - 3, :], x_t[:, m - 3, :]).then_inc(s_spill, 16)
            def store_c():
                sp.wait_ge(s_fa, 3)
                sp.dma_start(c_dram[:, 0, :], pt_hi[0:NH, :, :].bitcast(F32)).then_inc(s_cst, 16)
                sp.wait_ge(s_f, 7)
                sp.dma_start(c_dram[:, 1, :], pt_lo[0:NH, :, :].bitcast(F32)).then_inc(s_cst, 16)
                sp.wait_ge(s_fa, 4)
                sp.dma_start(c_dram[:, 2, :], v_st[0:NH, 0, :, :].bitcast(F32)).then_inc(s_cst, 16)
                sp.wait_ge(s_fa, 5)
                sp.dma_start(c_dram[:, 3, :], v_st[0:NH, 1, :, :].bitcast(F32)).then_inc(s_cst, 16)

            def c_rows(side, pair):
                own = P // 2 * (1 - side)
                head = 2 * pair + side
                sp.dma_start(q2[own:own + 2, side, :].bitcast(F32), c_dram[bass.ds(head, 1), 0:2, :]
                             .rearrange("a c s -> (a c) s")).then_inc(s_crow[side], 16)
                sp.dma_start(k2[own + 2:own + 4, side, :].bitcast(F32), c_dram[bass.ds(head, 1), 2:4, :]
                             .rearrange("a c s -> (a c) s")).then_inc(s_crow[side], 16)

            def iteration(it, proj, att):
                pair = it - 1
                if att:
                    if counted(16 * pair):
                        sp.wait_ge(s_sc, 16 * pair)
                    c_rows(1, pair)
                if proj:
                    n = N_AIN + 4 * it
                    for t in range(4):
                        m = n + 2 + t
                        if not isinstance(it, int) or 4 * it + t + 2 < 4 * PAIRS:
                            load_w(w_ain, m, (N_AIN + t) % 2, 4 * it + t + 2)
                        else:
                            load_w(w_aout, m, (N_AIN + t) % 2, t - 2)
                        if t == 2:
                            if counted(16 * pair + 8):
                                sp.wait_ge(s_sc, 16 * pair + 8)
                            if isinstance(it, int) and it == 0:
                                continue
                            c_rows(0, it)
                    if isinstance(it, int) and it == 0:
                        store_c()
                        sp.wait_ge(s_cst, 64)
                        sp.wait_ge(s_clear, 2)
                        c_rows(0, it)

            iteration(0, True, False)
            iteration(1, True, True)
            with sp.Fori(2, PAIRS - 1) as it:
                iteration(it, True, True)
            iteration(PAIRS - 1, True, True)
            iteration(PAIRS, False, True)
            def load_x1(m):
                if m == 0:
                    sp.wait_ge(s_spill, 16 * KT)
                    sp.wait_ge(s_qhi, 2 * PAIRS)
                    sp.wait_ge(s_stq, 2 * PAIRS)
                elif m == 1:
                    sp.wait_ge(s_khi, 2 * PAIRS)
                    sp.wait_ge(s_stk, 2 * PAIRS)
                elif m < AHEAD + 2:
                    sp.wait_ge(s_pre, 2 * (m - 2) + 2)
                else:
                    sp.wait_ge(s_or, 2 * (m - 2 - AHEAD) + 2)
                sp.dma_start((qn, kn)[m % 2][:, :], x1_dram[:, m, :]).then_inc(s_x1r[m % 2], 16)

            load_w(w_aout, N_AOUT + 2, N_AOUT % 2, 2)
            load_x1(0)
            load_x1(1)
            for m in range(2, AHEAD + 2):
                load_w(w_aout, N_AOUT + m + 1, (N_AOUT + m + 1) % 2, m + 1)
                load_x1(m)
            load_w(w_aout, N_AOUT + KT - 1, (N_AOUT + KT - 1) % 2, KT - 1)

            def store_out(m):
                if m < AHEAD:
                    sp.wait_ge(s_fin, 2 * m + 2)
                else:
                    sp.wait_ge(s_or, 2 * (m - AHEAD) + 2)
                sp.dma_start(out[:, m, :], y2[:, m, :]).then_inc(s_out, 16)

            store_out(AHEAD)
            load_x1(AHEAD + 2)
            for m in range(AHEAD):
                store_out(m)
            store_out(AHEAD + 1)
            load_x1(AHEAD + 3)
            for m in range(AHEAD + 2, KT - 1):
                store_out(m)
            for h in range(2):
                sp.wait_ge(s_or, 2 * (KT - 1 - AHEAD) + h + 1)
                sp.dma_start(out[:, KT - 1, halves(h)], y2[:, KT - 1, halves(h)]).then_inc(s_out, 16)
            sp.wait_ge(s_out, 16 * (KT + 1))

        @block.tensor
        def _(pe):
            mm = nc.tensor.matmul

            def unit_part(slot, bank, h, ks, mov_hi, mov_lo, ready=None, first=0, step=0, end=KT - 1):
                last = None
                for k in ks:
                    if ready is not None:
                        pe.wait_ge(ready, first + step * k)
                    for st, mov in ((w_hi, mov_hi), (w_hi, mov_lo), (w_lo, mov_hi)):
                        last = mm(ps[:, bank, :], st[:, slot, k, :], mov[:, k, halves(h)],
                                  start=(k == 0 and st is w_hi and mov is mov_hi),
                                  stop=(k == end and st is w_lo))
                return last

            def mean_square(turn, h):
                mm(ps[:, 6 + h, :], mean_d[:, :], acc[:, halves(h)], start=True, stop=True)\
                    .then_inc(s_ms, 1)

            def conv_block(j, first):
                for t in range(4):
                    n = 4 * j + t
                    if first and t == 2:
                        pe.wait_ge(s_vconst, 1)
                        pe.wait_ge(s_sqa, KT)
                        mean_square(0, 0)
                        pe.wait_ge(s_sq1, KT)
                        mean_square(0, 1)
                    pe.wait_ge(s_wlo, n + 1)
                    for h in range(2):
                        u = 2 * t + h
                        if first:
                            if t == 3:
                                pe.wait_ge(s_msr, h + 1)
                        else:
                            pe.wait_ge(s_evac, 8 * j + u - 7)
                        unit_part(t % 2, u, h, range(KT), h_hi, h_lo,
                                  s_h if first and t == 0 else None, KT * h + 1, 1).then_inc(s_unit, 1)

            conv_block(0, True)
            with pe.Fori(1, KT) as j:
                conv_block(j, False)

            with pe.Fori(0, 2) as i:
                for t in range(4):
                    pe.wait_ge(s_wlo, N_COUT + 4 * i + t + 1)
                    for h in range(2):
                        u = 2 * t + h
                        pe.wait_ge(s_evac, 8 * KT + 8 * i + u - 7)
                        unit_part(t % 2, u, h, range(KT), y_hi, y_lo,
                                  s_ylo if t == 0 else None, h + 1, 2).then_inc(s_unit, 1)

            pe.wait_ge(s_wlo, N_FORGET + 1)
            for h in range(2):
                pe.wait_ge(s_evac, 10 * KT - 8 + 4 + h + 1)
                unit_part(0, 4 + h, h, range(KT), h_hi, h_lo,
                          s_h, 2 * KT + h + 1, 2).then_inc(s_unit, 1)
                if h == 0:
                    pe.wait_ge(s_evac, 10 * KT)
                    pe.wait_ge(s_sqa, 3 * KT - 1)
                    mean_square(1, 0)
                    pe.wait_ge(s_sqa, 3 * KT)
                    mean_square(1, 1)

            def scores(it, i, par):
                pair = it - 1
                side, t = STEPS[i]
                if t == 3 and par == 0:
                    pe.wait_ge(s_qhi, 2 * pair + side + 1)
                    pe.wait_ge(s_khi, 2 * pair + side + 1)
                    pe.wait_ge(s_stq, 2 * pair + side + 1)
                    pe.wait_ge(s_stk, 2 * pair + side + 1)
                    pe.wait_ge(s_crow[side], 32 * pair + 32)
                if counted(16 * pair + 2 * i + (par if t >= 2 else 0 if t == 1 else par - 1)):
                    pe.wait_ge(s_exp, 16 * pair + 2 * i + (par if t >= 2 else 0 if t == 1 else par - 1))
                qs = (2 * t + par) * P
                n, w = (2, P * (t + 1)) if t >= 2 else (1, 2 * P * (t + 1))
                skip = P if par == 0 and t else 0
                for c in range(n):
                    bank = B_SCORE + (c if t >= 2 else par)
                    last_c = c == n - 1
                    used = w - skip if last_c else w
                    for a, b in ((q1, k1), (q2, k2)):
                        last = mm(ps[:, bank, 0:used], a[:, side, qs:qs + P],
                                  b[:, side, c * w:c * w + used],
                                  start=(a is q1), stop=(a is q2 and not last_c))
                    if last_c:
                        lo = 2 * P * t - c * w + par * P
                        mw = 2 * P - par * P - skip
                        last = mm(ps[:, bank, lo:lo + mw], ident_bf[:, :], mask_bf[:, 0:mw],
                                  start=False, stop=True)
                        if skip:
                            last = mm(ps[:, bank, used:w], ident_bf[:, :], mask_bf[:, P:2 * P],
                                      start=True, stop=True)
                last.then_inc(s_sc, 1)

            def transpose_p(it, i, c):
                pair = it - 1
                t = STEPS[i][1]
                g = CHUNK0[i] + c
                if c == 0:
                    pe.wait_ge(s_pn, 16 * pair + 2 * i + 2)
                if counted(CHUNKS * pair + g - 1):
                    pe.wait_ge(s_ptl, CHUNKS * pair + g - 1)
                src = p_big if i % 2 == 0 else p_small
                for kp in range(2):
                    for par in range(2):
                        at = (2 * kp + par) * P
                        last = nc.tensor.transpose(ps[:, B_PT + g % 2, at:at + P],
                                                   src[:, par, (2 * c + kp) * P:(2 * c + kp + 1) * P],
                                                   ident[:, :])
                last.then_inc(s_ptr, 1)

            def pv(it, i, c):
                pair = it - 1
                side, t = STEPS[i]
                g = CHUNK0[i] + c
                if c == 0 and t % 2 == 1:
                    if counted(4 * pair + 2 * side + (0 if t == 3 else 1)):
                        pe.wait_ge(s_os, 4 * pair + 2 * side + (0 if t == 3 else 1))
                    pe.wait_ge(s_vlo, 2 * pair + side + 1)
                pe.wait_ge(s_ptl, CHUNKS * pair + g + 1)
                at = (t % 2) * 2 * P
                for kp in range(2):
                    for mov in (pt_hi, pt_lo):
                        last = mm(ps[:, B_OUT, at:at + 2 * P], v_st[:, side, 2 * c + kp, :],
                                  mov[:, g % 2, kp * 2 * P:(kp + 1) * 2 * P],
                                  start=(c == 0 and kp == 0 and mov is pt_hi),
                                  stop=(c == t and kp == 1 and mov is pt_lo))
                last.then_inc(s_pv, 1)

            def head_square(it, u):
                if u == 0:
                    if counted(2 * it):
                        pe.wait_ge(s_vlo, 2 * it)
                if counted(4 * it + u):
                    pe.wait_ge(s_qkn, 4 * it + u)
                pe.wait_ge(s_sql, 4 * it + u + 1)
                mm(ps[:, B_MISC, :], mean_h[:, :], sq_hi[:, :], start=True, stop=False)
                mm(ps[:, B_MISC, :], mean_h[:, :], sq_lo[:, :], start=False, stop=True).then_inc(s_ssq, 1)

            def transpose_v(side):
                r = DH * side
                for k in range(KT):
                    last = nc.tensor.transpose(ps[:, B_MISC, k * DH:(k + 1) * DH],
                                               v_t[r:r + DH, k * P:(k + 1) * P],
                                               ident[r:r + DH, r:r + DH])
                last.then_inc(s_vtr, 1)

            def unit_start(it, i):
                if i % 2 == 0:
                    pe.wait_ge(s_wlo, N_AIN + 4 * it + i // 2 + 1)
                if i < 2:
                    if counted(4 * it - 1 + i):
                        pe.wait_ge(s_vz, 4 * it - 1 + i)
                elif i < 6:
                    pe.wait_ge(s_qkraw, 4 * it + i - 1)
                else:
                    pe.wait_ge(s_vz, 4 * it + i - 5)

            def piece(it, i, p):
                if p == 0:
                    unit_start(it, i)
                last = unit_part((N_AIN + i // 2) % 2, B_PROJ + i % 2, i % 2, [p], h_hi, h_lo)
                if p == KT - 1:
                    last.then_inc(s_unit, 1)

            def out_ahead(f):
                u, k = divmod(f, KT - 1)
                m, h = divmod(u, 2)
                if k == 0:
                    pe.wait_ge(s_wlo, N_AOUT + m + 1)
                    if u < 2:
                        pe.wait_ge(s_vz, 4 * PAIRS)
                    else:
                        pe.wait_ge(s_pre, u - 1)
                if u == 0:
                    if k % 2 == 0:
                        pe.wait_ge(s_y2v, k // 2 + 1)
                    else:
                        pe.wait_ge(s_y2l, k // 2 + 1)
                last = unit_part((N_AOUT + m) % 2, B_PROJ + u % 2, h, [k], h_hi, h_lo, end=KT - 2)
                if k == KT - 2:
                    last.then_inc(s_unit, 1)

            def pieces(it, i, proj, ps_):
                for p in ps_:
                    if proj:
                        piece(it, i, p)
                    elif KT * (i - 1) + p >= KT // 2:
                        out_ahead(KT * (i - 1) + p - KT // 2)

            def iteration(it, proj, att, before):
                for i in range(8):
                    own, at = (it, i - 1) if i else (it - 1, 7)
                    chunks = STEPS[at][1] + 1 if (att and i) or (before and not i) else 0
                    if att:
                        scores(it, i, 0)
                    if att and i == 1:
                        pe.wait_ge(s_vlo, 2 * it - 1)
                    pieces(it, i, proj, (0, 1))
                    if att and i == 1:
                        transpose_v(1)
                    for c in range(min(2, chunks)):
                        transpose_p(own, at, c)
                    pieces(it, i, proj, (2,))
                    if att and i == 0:
                        pe.wait_ge(s_vz, 4 * it)
                        pe.wait_ge(s_qkn, 4 * it)
                    pieces(it, i, proj, (3,))
                    if proj and 2 <= i <= 5:
                        head_square(it, i - 2)
                    if att and i == 0:
                        transpose_v(0)
                    if att:
                        scores(it, i, 1)
                    for c in range(4):
                        if c < chunks:
                            pv(own, at, c)
                        if c + 2 < chunks:
                            transpose_p(own, at, c + 2)
                        pieces(it, i, proj, (4 + c,))

            pe.wait_ge(s_ident, 3)
            iteration(0, True, False, False)
            iteration(1, True, True, False)
            with pe.Fori(2, PAIRS) as it:
                iteration(it, True, True, True)
            iteration(PAIRS, False, True, True)

            def out_bank(m, h):
                return (B_PROJ, B_PROJ + 1, B_OUT, B_MISC)[(2 * m + h) % 4]

            def out_unit(m, h, ks):
                unit_ks = unit_part((N_AOUT + m) % 2, out_bank(m, h), h, ks, h_hi, h_lo)
                if ks[-1] == KT - 1:
                    unit_ks.then_inc(s_unit, 1)

            for f in range(2 * AHEAD * (KT - 1) - KT // 2, 2 * AHEAD * (KT - 1)):
                out_ahead(f)
            pe.wait_ge(s_wlo, N_AOUT + AHEAD + 1)
            pe.wait_ge(s_pre, 2 * AHEAD - 1)
            out_unit(AHEAD, 0, range(0, 4))
            transpose_p(PAIRS, 7, 0)
            out_unit(AHEAD, 0, range(4, KT - 1))
            pv(PAIRS, 7, 0)
            pe.wait_ge(s_pre, 2 * AHEAD)
            out_unit(AHEAD, 1, range(0, KT - 1))
            for h in range(2):
                pe.wait_ge(s_y2v, KT // 2 + h + 1)
                out_unit(AHEAD, h, [KT - 1])
            pe.wait_ge(s_exp, 16 * PAIRS)
            pe.wait_ge(s_ptl, CHUNKS * PAIRS)
            pe.wait_ge(s_w7, AHEAD)
            for u in range(2 * AHEAD):
                m, h = divmod(u, 2)
                if counted(u - 3):
                    pe.wait_ge(s_fin, u - 3)
                for st, mov in ((w7_hi, h_hi), (w7_hi, h_lo), (w7_lo, h_hi)):
                    last = mm(ps[:, B_SCORE + u % 4, :], st[:, m, :], mov[:, KT - 1, halves(h)],
                              start=(st is w7_hi and mov is h_hi), stop=(st is w7_lo))
                last.then_inc(s_tail, 1)
            for m in range(AHEAD + 1, KT):
                pe.wait_ge(s_wlo, N_AOUT + m + 1)
                for h in range(2):
                    if m == AHEAD + 1:
                        pe.wait_ge(s_os, 4 * PAIRS)
                        pe.wait_ge(s_vlo, 2 * PAIRS)
                    else:
                        pe.wait_ge(s_or, 2 * (m - AHEAD) + h - 3)
                    out_unit(m, h, range(KT))

        @block.scalar
        def _(act):
            A = nc.scalar.activation

            def split_w(n, slot, turn):
                act.wait_ge(s_wraw[slot], 16 * turn + 16)
                if counted(2 * n - 2):
                    act.wait_ge(s_unit, 2 * n - 2)
                A(w_hi[:, slot, :, :], w_raw[:, slot, :, :], ACT.Copy).then_inc(s_whi, 1)

            act.dma_start(g1[:, :], conv_gain).then_inc(s_g1, 16)

            def gained(c):
                h, k = divmod(c, KT)
                if c % 2 == 0:
                    act.wait_ge(s_x[c // 2], 16)
                A(h_hi[:, k, halves(h)], x_t[:, k, halves(h)], ACT.Copy, scale=g1[:, k:k + 1])\
                    .then_inc(s_hh, 1)

            def squared(c):
                h, k = divmod(c, KT)
                if h == 0 and k >= 2:
                    act.wait_ge(s_sqa, k - 1)
                if h == 1 and k >= 2:
                    act.wait_ge(s_sq1, k - 1)
                A((sq2, mbuf)[h][:, halves(k % 2)], x_t[:, k, halves(h)], ACT.Square).then_inc(s_sqm, 1)

            split_w(0, 0, 0)
            act.wait_ge(s_g1, 16)
            for c in range(KT):
                gained(c)
            squared(0)
            squared(1)
            split_w(1, 1, 0)
            for c in range(4):
                gained(KT + 2 * c)
                gained(KT + 2 * c + 1)
                squared(2 + c)
            for c in range(6, 2 * KT):
                squared(c)
            split_w(2, 0, 1)

            def rsqrt_guess(turn):
                act.wait_ge(s_msr, 2 * turn + 2)
                A(inv[:, :], mbuf, ACT.Ln).then_inc(s_rs0, 1)
                act.wait_ge(s_rs0, 2 * turn + 1)
                A(inv[:, :], inv[:, :], ACT.Exp, scale=-0.5).then_inc(s_rs0, 1)

            nc.scalar.preload_act_table_set("natural_log_exp_and_others")
            rsqrt_guess(0)

            def conv_block(j, first):
                for t in range(4):
                    if not first or t > 1:
                        split_w(4 * j + t + 1, (t + 1) % 2, 2 * j + (t + 1) // 2)
                for h in range(2):
                    act.wait_ge(s_evac, 8 * j + 4 + h + 1)
                    A(gate[:, halves(h)], gate[:, halves(h)], ACT.Silu).then_inc(s_gate, 1)
                for h in range(2):
                    act.wait_ge(s_y, 2 * j + h + 1)
                    A(y_hi[:, j, halves(h)], yb[:, halves(h)], ACT.Copy).then_inc(s_yhi, 1)

            conv_block(0, True)
            with act.Fori(1, KT) as j:
                conv_block(j, False)

            with act.Fori(0, 2) as i:
                for t in range(4):
                    split_w(N_COUT + 4 * i + t + 1, (t + 1) % 2, 2 * KT + 2 * i + (t + 1) // 2)
                    for h in range(2):
                        u = 8 * i + 2 * t + h
                        act.wait_ge(s_evac, 8 * KT + u + 1)
                        act.wait_ge(s_sqa, KT + u - 1)
                        A(sq2[:, halves(h)], x_t[:, 4 * i + t, halves(h)], ACT.Square)\
                            .then_inc(s_sqm, 1)

            nc.scalar.preload_act_table_set("natural_log_exp_and_others")
            split_w(N_AIN, 1, N_AIN // 2)
            rsqrt_guess(1)
            def forget(part):
                f = p_big[0:NH, 0, :]
                if part == 0:
                    act.wait_ge(s_f, 4)
                    A(f, f, ACT.Exp).then_inc(s_fa, 1)
                    act.wait_ge(s_fa, 1)
                    A(f, f, ACT.Ln, bias=1.0).then_inc(s_fa, 1)
                if part == 1:
                    act.wait_ge(s_f, 6)
                    A(pt_hi[0:NH, :, :], f.rearrange("p (a n) -> p a n", a=2), ACT.Copy).then_inc(s_fa, 1)
                if part == 2:
                    act.wait_ge(s_fa, 3)
                    act.wait_ge(s_f, 7)
                    A(v_st[0:NH, 0, :, :], pt_hi[0:NH, :, :].bitcast(F32).rearrange("p a n -> p (a n)"),
                      ACT.Copy, scale=-1.0).then_inc(s_fa, 1)
                    A(v_st[0:NH, 1, :, :], pt_lo[0:NH, :, :].bitcast(F32).rearrange("p a n -> p (a n)"),
                      ACT.Copy, scale=-1.0).then_inc(s_fa, 1)

            def softmax_exp(it, i, par):
                pair = it - 1
                t = STEPS[i][1]
                w = 2 * P * (t + 1)
                col = 2 * (i % 2) + par
                act.wait_ge(s_max, 16 * pair + 2 * i + par + 1)
                if counted(CHUNKS * pair + (CHUNK0[i - 1] if i else 0) - (1 if i == 0 else 0)):
                    act.wait_ge(s_ptr, CHUNKS * pair + (CHUNK0[i - 1] if i else 0) - (1 if i == 0 else 0))
                if counted(16 * pair + 2 * i + par - 3):
                    act.wait_ge(s_rd, 16 * pair + 2 * i + par - 3)
                dst = (p_big if i % 2 == 0 else p_small)[:, par, 0:w]
                if t >= 2:
                    src = ps[:, B_SCORE:B_SCORE + 2, 0:w // 2]
                    dst = dst.rearrange("p (b n) -> p b n", b=2)
                else:
                    src = ps[:, B_SCORE + par, 0:w]
                A(dst, src, ACT.Exp, bias=neg_max[:, col:col + 1],
                  accum_out=denom[:, col:col + 1]).then_inc(s_exp, 1)

            def pt_split(it, g):
                pair = it - 1
                act.wait_ge(s_ptr, CHUNKS * pair + g + 1)
                if counted(CHUNKS * pair + g - 1):
                    act.wait_ge(s_pv, CHUNKS * pair + g - 1)
                A(pt_hi[:, g % 2, :], ps[:, B_PT + g % 2, :], ACT.Copy).then_inc(s_pth, 1)

            def out_copy(it, i):
                pair = it - 1
                side, t = STEPS[i]
                r = DH * side
                act.wait_ge(s_pv, CHUNKS * pair + CHUNK0[i] + t + 1)
                if counted(4 * pair + 2 * side + (0 if t == 2 else 1)):
                    act.wait_ge(s_y2, 4 * pair + 2 * side + (0 if t == 2 else 1))
                A(osum[r:r + DH, :], ps[DH:P, B_OUT, :], ACT.Copy).then_inc(s_oc, 1)

            def stack_q_hi(pair, side):
                own = slice(DH * side, DH * side + DH)
                act.wait_ge(s_qkn, 4 * pair + 2)
                if counted(16 * pair - 8 + 8 * side):
                    act.wait_ge(s_sc, 16 * pair - 8 + 8 * side)
                act.wait_ge(s_clear, 2)
                A(q1[own, side, :], qn[own, :], ACT.Copy)
                A(q2[own, side, :], qn[own, :], ACT.Copy).then_inc(s_qhi, 1)

            def stack_k_hi(pair, side):
                own = slice(DH * side, DH * side + DH)
                other = slice(DH * (1 - side), DH * (1 - side) + DH)
                act.wait_ge(s_qkn, 4 * pair + 4)
                if counted(16 * pair - 8 + 8 * side):
                    act.wait_ge(s_sc, 16 * pair - 8 + 8 * side)
                A(k1[own, side, :], kn[own, :], ACT.Copy)
                A(k1[other, side, :], kn[own, :], ACT.Copy).then_inc(s_khi, 1)

            def v_split(pair, side):
                act.wait_ge(s_vtr, 2 * pair + side + 1)
                if counted(CHUNKS * pair - 10 + 10 * side):
                    act.wait_ge(s_pv, CHUNKS * pair - 10 + 10 * side)
                act.wait_ge(s_cst, 64)
                A(v_st[:, side, :, 0:DH], ps[:, B_MISC, :].rearrange("p (k d) -> p k d", d=DH),
                  ACT.Copy).then_inc(s_vhi, 1)

            def iteration(it, proj, att, before):
                for i in range(8):
                    own, at = (it, i - 1) if i else (it - 1, 7)
                    chunks = STEPS[at][1] + 1 if (att and i) or (before and not i) else 0
                    if proj and i % 2 == 0:
                        n = N_AIN + 4 * it + i // 2 + 1
                        split_w(n, (N_AIN + i // 2 + 1) % 2, 2 * it + (N_AIN + i // 2 + 1) // 2)
                    if not proj and i in (4, 5, 7):
                        m = (4, 5, 7).index(i)
                        w7_copy(m)
                        split_w(N_AOUT + m + 2, (N_AOUT + m) % 2, (N_AOUT + m + 2) // 2)
                    if att:
                        softmax_exp(it, i, 0)
                    for c in range(min(2, chunks)):
                        pt_split(own, CHUNK0[at] + c)
                    if att and i == 0:
                        v_split(it - 1, 0)
                        if proj:
                            stack_q_hi(it - 1, 1)
                    if not proj and i == 0:
                        for k in range(3):
                            y2_split(k, None)
                    if att and i == 1:
                        v_split(it - 1, 1)
                        if proj:
                            stack_k_hi(it - 1, 1)
                    if not proj and i == 1:
                        y2_split(4, None)
                    if not proj and i == 2:
                        stack_k_hi(it - 1, 1)
                    if proj and 2 <= i <= 5:
                        guess(it, i - 2)
                    if not att and i in (3, 5, 6):
                        forget((3, 5, 6).index(i))
                    if proj and i == (6 if att else 5):
                        stack_q_hi(it, 0)
                    if chunks > 2:
                        pt_split(own, CHUNK0[at] + 2)
                    if att:
                        softmax_exp(it, i, 1)
                    if chunks > 3:
                        pt_split(own, CHUNK0[at] + 3)
                    if proj and 1 <= i <= 4:
                        square(it, i - 1)
                    if proj and i == 7:
                        z_silu(it)
                    if proj and i == 6:
                        stack_k_hi(it, 0)
                    if not proj and i == 0:
                        y2_split(3, None)
                    if not proj and i == 1:
                        y2_split(5, None)
                        stack_q_hi(it - 1, 1)
                        y2_split(6, None)
                        split_w(N_AOUT + 1, (N_AOUT + 1) % 2, (N_AOUT + 1) // 2)
                    if chunks and STEPS[at][1] % 2 == 0:
                        out_copy(own, at)

            def guess(it, u):
                act.wait_ge(s_ssq, 4 * it + u + 1)
                if counted(4 * it + u):
                    act.wait_ge(s_qkn, 4 * it + u)
                A(y0[:, :], ps[:, B_MISC, :], ACT.Ln, bias=eps_col[:, :]).then_inc(s_guess, 1)
                act.wait_ge(s_guess, 8 * it + 2 * u + 1)
                A(y0[:, :], y0[:, :], ACT.Exp, scale=-0.5).then_inc(s_guess, 1)

            def square(it, u):
                act.wait_ge(s_qkraw, 4 * it + u + 1)
                if counted(4 * it + u):
                    act.wait_ge(s_ssq, 4 * it + u)
                A(sq_hi[:, :], (qn, kn)[u // 2][:, halves(u % 2)], ACT.Square).then_inc(s_qsq, 1)

            def z_silu(it):
                act.wait_ge(s_vz, 4 * it + 2)
                A(y2[:, it, :], y2[:, it, :], ACT.Silu).then_inc(s_gz, 1)
                nc.scalar.preload_act_table_set("natural_log_exp_and_others")

            def w7_copy(m):
                act.wait_ge(s_vz, 4 * PAIRS)
                act.wait_ge(s_wlo, N_AOUT + m + 1)
                slot = (N_AOUT + m) % 2
                A(w7_hi[:, m, :], w_hi[:, slot, KT - 1, :].bitcast(F32), ACT.Copy)
                A(w7_lo[:, m, :], w_lo[:, slot, KT - 1, :].bitcast(F32), ACT.Copy).then_inc(s_w7, 1)
                act.wait_ge(s_w7, m + 1)

            def y2_split(k, h):
                cols = slice(0, S) if h is None else halves(h)
                act.wait_ge(s_unit, 2 * N_AOUT)
                act.wait_ge(s_y2, 4 * k + 4)
                A(h_hi[:, k, cols], y2[:, k, cols], ACT.Copy).then_inc(s_y2h, 1)

            iteration(0, True, False, False)
            iteration(1, True, True, False)
            with act.Fori(2, PAIRS) as it:
                iteration(it, True, True, True)
            iteration(PAIRS, False, True, True)
            pt_split(PAIRS, CHUNK0[7])
            out_copy(PAIRS, 7)
            y2_split(KT - 1, 0)
            y2_split(KT - 1, 1)

            w7_copy(AHEAD - 1)
            for n in range(N_AOUT + AHEAD + 1, N_TILES):
                split_w(n, n % 2, n // 2)

        @block.vector
        def _(dve):
            v = nc.vector
            TT, TS, STT = v.tensor_tensor, v.tensor_scalar, v.scalar_tensor_tensor
            steps = [0]

            def own(ins):
                steps[0] += 1
                ins.then_inc(s_dve, 1)
                dve.wait_ge(s_dve, steps[0])

            v.memset(mean_d[:, :], 1.0 / D)
            v.memset(eps_col[:, :], EPS)
            for a in range(2):
                for b in range(2):
                    v.memset(mean_h[a * DH:(a + 1) * DH, b * DH:(b + 1) * DH].bitcast(F32), 1.0 / DH if a == b else 0.0)
            v.memset(mask_bf[:, 0:P], 0.0)
            v.memset(mask_bf[:, P:2 * P], MASKED).then_inc(s_vconst, 1)
            dve.wait_ge(s_g1, 16)
            for c in range(2 * KT):
                h, k = divmod(c, KT)
                dve.wait_ge(s_hh, c + 1)
                STT(h_lo[:, k, halves(h)], x_t[:, k, halves(h)], g1[:, k:k + 1],
                    h_hi[:, k, halves(h)].bitcast(F32), ALU.mult, ALU.subtract).then_inc(s_h, 1)
            dve.wait_ge(s_zero, 1)
            for k in range(KT):
                dve.wait_ge(s_sqm, KT + k + 1)
                if k:
                    dve.wait_ge(s_sq1, k)
                TT(acc[:, halves(1)], acc[:, halves(1)], mbuf[:, halves(k % 2)], ALU.add).then_inc(s_sq1, 1)
            dve.wait_ge(s_const, 16 * 7)
            dve.wait_ge(s_sq1, KT)
            own(TS(gq[:, :], gq[:, :], -0.5 / DH ** 0.5, None, ALU.mult))
            own(TS(gk[:, :], gk[:, :], -0.5, None, ALU.mult))

            def rsqrt(turn):
                for h in range(2):
                    dve.wait_ge(s_ms, 2 * turn + h + 1)
                    TS(mbuf[:, halves(h)], ps[:, 6 + h, :], EPS, None, ALU.add).then_inc(s_msr, 1)
                dve.wait_ge(s_rs0, 2 * turn + 2)
                t = ubuf[:, 0:S]
                own(TT(t, inv[:, :], inv[:, :], ALU.mult))
                own(STT(t, t, -0.5, mbuf, ALU.mult, ALU.mult))
                own(STT(inv[:, :], t, 1.5, inv[:, :], ALU.add, ALU.mult))
                return v.memset(ubuf[:, 0:2], 0.0).then_inc(s_inv, 1)

            rsqrt(0)
            dve.wait_ge(s_inv, 1)

            with dve.Fori(0, KT) as j:
                base = steps[0] + j * 8
                local = 0
                for t in range(4):
                    for h in range(2):
                        u = 2 * t + h
                        hs = halves(h)
                        dve.wait_ge(s_unit, 8 * j + u + 1)
                        if t == 0:
                            TT(ca[:, hs], ps[:, u, :], inv[:, hs], ALU.mult).then_inc(s_evac, 1)
                        if t == 1:
                            dve.wait_ge(s_evac, 8 * j + h + 1)
                            TT(ubuf[:, 2 + h * HALF:2 + (h + 1) * HALF], ps[:, u, :], ca[:, hs],
                               ALU.mult).then_inc(s_evac, 1)
                            dve.wait_ge(s_u, 2 * j + h + 1)
                            for i in range(TAPS):
                                w = taps[:, TAPS - 1 - i, bass.ds(j, 1)]
                                us = ubuf[:, 2 + h * HALF - i:2 + (h + 1) * HALF - i]
                                if i == 0:
                                    ins = TS(ca[:, hs], us, w, None, ALU.mult)
                                else:
                                    ins = STT(ca[:, hs], us, w, ca[:, hs], ALU.mult, ALU.add)
                                local += 1
                                ins.then_inc(s_dve, 1)
                                dve.wait_ge(s_dve, base + local)
                        if t == 2:
                            TT(gate[:, hs], ps[:, u, :], inv[:, hs], ALU.mult).then_inc(s_evac, 1)
                        if t == 3:
                            TT(yb[:, hs], ps[:, u, :], inv[:, hs], ALU.mult).then_inc(s_evac, 1)
                            dve.wait_ge(s_evac, 8 * j + u + 1)
                            local += 1
                            TT(yb[:, hs], yb[:, hs], ca[:, hs], ALU.mult).then_inc(s_dve, 1)
                            dve.wait_ge(s_dve, base + local)
                            dve.wait_ge(s_gate, 2 * j + h + 1)
                            TT(yb[:, hs], yb[:, hs], gate[:, hs], ALU.mult).then_inc(s_y, 1)
                            dve.wait_ge(s_yhi, 2 * j + h + 1)
                            TT(y_lo[:, j, hs], yb[:, hs],
                               y_hi[:, j, hs].bitcast(F32), ALU.subtract).then_inc(s_ylo, 1)
                assert local == 8
            steps[0] += 8 * KT

            with dve.Fori(0, 2) as i:
                base = steps[0] + i * 8
                for t in range(4):
                    for h in range(2):
                        u = 2 * t + h
                        hs = halves(h)
                        m = 4 * i + t
                        gain = g2[:, bass.ds(m, 1)]
                        dve.wait_ge(s_unit, 8 * KT + 8 * i + u + 1)
                        TT(x_t[:, m, hs], ps[:, u, :], x_t[:, m, hs], ALU.add).then_inc(s_evac, 1)
                        dve.wait_ge(s_evac, 8 * KT + 8 * i + u + 1)
                        TS(h_hi[:, m, hs], x_t[:, m, hs], gain, None, ALU.mult).then_inc(s_dve, 1)
                        dve.wait_ge(s_dve, base + u + 1)
                        STT(h_lo[:, m, hs], x_t[:, m, hs], gain, h_hi[:, m, hs].bitcast(F32),
                            ALU.mult, ALU.subtract).then_inc(s_h, 1)
            steps[0] += 16

            def set_stacks(value, rows):
                for side in range(2):
                    r = DH * (1 - side)
                    for st in (q2, k2):
                        ins = v.memset(st[r:r + rows, side, :].bitcast(F32), value)
                ins.then_inc(s_clear, 1)

            dve.wait_ge(s_unit, 2 * N_FORGET)
            set_stacks(0.0, DH)
            rsqrt(1)
            dve.wait_ge(s_inv, 2)

            def forget(part):
                f, m0, ones = p_big[0:NH, 0, :], p_big[0:NH, 1, :], y2[0:NH, KT - 1, :]
                if part == 0:
                    for h in range(2):
                        dve.wait_ge(s_unit, 2 * N_FORGET + h + 1)
                        ins = TT(f[:, halves(h)], ps[0:NH, 4 + h, :], inv[0:NH, halves(h)], ALU.mult)
                    ins.then_inc(s_f, 1)
                    dve.wait_ge(s_f, 1)
                    TS(f, f, b_f[:, :], None, ALU.add).then_inc(s_f, 1)
                    dve.wait_ge(s_f, 2)
                    TS(m0, f, 0.0, None, ALU.min).then_inc(s_f, 1)
                    dve.wait_ge(s_f, 3)
                    STT(f, m0, 2.0, f, ALU.mult, ALU.subtract).then_inc(s_f, 1)
                if part == 1:
                    dve.wait_ge(s_spill, 16 * KT)
                    v.memset(ones, 1.0)
                    dve.wait_ge(s_fa, 2)
                    TT(m0, m0, f, ALU.subtract).then_inc(s_f, 1)
                    dve.wait_ge(s_f, 5)
                    v.tensor_tensor_scan(f, ones, m0, 0.0, ALU.mult, ALU.add).then_inc(s_f, 1)
                if part == 2:
                    dve.wait_ge(s_fa, 3)
                    TT(pt_lo[0:NH, :, :].rearrange("p a n -> p (a n)"), f,
                       pt_hi[0:NH, :, :].bitcast(F32).rearrange("p a n -> p (a n)"), ALU.subtract)\
                        .then_inc(s_f, 1)

            def row_max(it, i, par):
                pair = it - 1
                t = STEPS[i][1]
                w = 2 * P * (t + 1)
                col = 2 * (i % 2) + par
                dve.wait_ge(s_sc, 16 * pair + 2 * i + par + 1)
                if t >= 2:
                    src, ax = ps[:, B_SCORE:B_SCORE + 2, 0:w // 2], AX.XY
                else:
                    src, ax = ps[:, B_SCORE + par, 0:w], AX.X
                v.tensor_reduce(neg_max[:, col:col + 1], src, ax, ALU.max, negate=True).then_inc(s_max, 1)

            def invert(it, i, par):
                pair = it - 1
                col = 2 * (i % 2) + par
                dve.wait_ge(s_exp, 16 * pair + 2 * i + par + 1)
                if counted(16 * pair + 2 * i + par - 3):
                    dve.wait_ge(s_pn, 16 * pair + 2 * i + par - 3)
                v.reciprocal(rdenom[:, col:col + 1], denom[:, col:col + 1]).then_inc(s_rd, 1)

            def pt_low(it, g):
                pair = it - 1
                dve.wait_ge(s_pth, CHUNKS * pair + g + 1)
                TT(pt_lo[:, g % 2, :], ps[:, B_PT + g % 2, :], pt_hi[:, g % 2, :].bitcast(F32),
                   ALU.subtract).then_inc(s_ptl, 1)

            def out_sum(it, i):
                side, t = STEPS[i]
                r = DH * side
                dve.wait_ge(s_oc, 4 * (it - 1) + 2 * side + (1 if t == 2 else 2))
                TT(osum[r:r + DH, :], ps[0:DH, B_OUT, :], osum[r:r + DH, :], ALU.add).then_inc(s_os, 1)

            def out_gate(it, i):
                pair = it - 1
                side, t = STEPS[i]
                r = DH * side
                dve.wait_ge(s_os, 4 * pair + 2 * side + (1 if t == 2 else 2))
                dve.wait_ge(s_gz, pair + 1)
                dst = y2[r:r + DH, pair, halves(1 if t == 2 else 0)]
                TT(dst, osum[r:r + DH, :], dst, ALU.mult).then_inc(s_y2, 1)

            def stack_q_lo(pair, side):
                o, r = DH * side, DH * (1 - side)
                dve.wait_ge(s_qhi, 2 * pair + side + 1)
                TT(q1[r:r + DH, side, :], qn[o:o + DH, :], q1[o:o + DH, side, :].bitcast(F32),
                   ALU.subtract).then_inc(s_stq, 1)

            def v_low(pair, side):
                dve.wait_ge(s_vhi, 2 * pair + side + 1)
                TT(v_st[:, side, :, DH:P], ps[:, B_MISC, :].rearrange("p (k d) -> p k d", d=DH),
                   v_st[:, side, :, 0:DH].bitcast(F32), ALU.subtract).then_inc(s_vlo, 1)

            NEWTON = 3

            def refine(it, u, base, local):
                dst = (qn, kn)[u // 2][:, halves(u % 2)]
                dve.wait_ge(s_guess, 8 * it + 2 * u + 2)
                if counted(2 * it):
                    dve.wait_ge(s_vtr, 2 * it)
                TT(newton[:, :], y0[:, :], y0[:, :], ALU.mult).then_inc(s_dve, 1)
                dve.wait_ge(s_dve, base + local + 1)
                STT(newton[:, :], ps[:, B_MISC, :], EPS, newton[:, :], ALU.add, ALU.mult).then_inc(s_dve, 1)
                dve.wait_ge(s_dve, base + local + 2)
                STT(newton[:, :], newton[:, :], 3.0, y0[:, :], ALU.subtract, ALU.mult).then_inc(s_dve, 1)
                dve.wait_ge(s_dve, base + local + 3)
                STT(dst, dst, (gq, gk)[u // 2][:, :], newton[:, :], ALU.mult, ALU.mult).then_inc(s_qkn, 1)
                return local + NEWTON

            def qk_evac(it, u):
                dve.wait_ge(s_unit, 2 * N_AIN + 8 * it + u + 1)
                if u < 2:
                    if counted(2 * it):
                        dve.wait_ge(s_stq, 2 * it)
                else:
                    if counted(2 * it):
                        dve.wait_ge(s_khi, 2 * it)
                        dve.wait_ge(s_stk, 2 * it)
                TT((qn, kn)[u // 2][:, halves(u % 2)], ps[:, B_PROJ + u % 2, :],
                   inv[:, halves(u % 2)], ALU.mult).then_inc(s_qkraw, 1)

            def vz_evac(it, u):
                h = u % 2
                dve.wait_ge(s_unit, 2 * N_AIN + 8 * it + u + 1)
                if u >= 6:
                    if counted(2 * it):
                        dve.wait_ge(s_vtr, 2 * it)
                    dve.wait_ge(s_qkn, 4 * it + 4)
                    dst = v_t[:, halves(h)]
                else:
                    dst = y2[:, it, halves(h)]
                TT(dst, ps[:, B_PROJ + h, :], inv[:, halves(h)], ALU.mult).then_inc(s_vz, 1)

            def iteration(it, proj, att, before, base):
                local = 0
                for i in range(8):
                    own, at = (it, i - 1) if i else (it - 1, 7)
                    chunks = STEPS[at][1] + 1 if (att and i) or (before and not i) else 0
                    if att:
                        row_max(it, i, 0)
                    if att and i and STEPS[i - 1][1] in (1, 3) and (i >= 2 or before):
                        out_gate(*((it, i - 2) if i >= 2 else (it - 1, 7)))
                    if att and i == 0:
                        vz_evac(it - 1, 7)
                    if proj and 1 <= i <= 4:
                        qk_evac(it, i - 1)
                    if proj and 5 <= i:
                        vz_evac(it, i - 1)
                    if not proj and i > 4:
                        add_ahead(i - 2)
                    if att:
                        invert(it, i, 0)
                    for c in range(min(2, chunks)):
                        pt_low(own, CHUNK0[at] + c)
                    if att and i == 0:
                        v_low(it - 1, 0)
                    if not proj and i == 0:
                        y2_low(0)
                    if att:
                        row_max(it, i, 1)
                    if not proj and i == 1:
                        y2_low(4)
                    if att and proj and i == 0:
                        stack_q_lo(it - 1, 1)
                    if att and i == 1:
                        v_low(it - 1, 1)
                    for c in range(2, chunks):
                        pt_low(own, CHUNK0[at] + c)
                    if not att and i == 1:
                        dve.wait_ge(s_clear, 1)
                        set_stacks(1.0, 4)
                    if att:
                        invert(it, i, 1)
                    if proj and 2 <= i <= 5:
                        local = refine(it, i - 2, base, local)
                    if not att and i in (2, 4, 5):
                        forget((2, 4, 5).index(i))
                    if proj and i == 7:
                        stack_q_lo(it, 0)
                    if not proj and i == 0:
                        y2_low(2)
                    if not proj and i == 1:
                        stack_q_lo(it - 1, 1)
                        y2_low(6)
                    if not proj and 2 <= i <= 4:
                        add_ahead(i - 2)
                    if chunks and STEPS[at][1] % 2 == 0:
                        out_sum(own, at)
                return local

            def y2_low(k):
                dve.wait_ge(s_y2h, k + 1)
                TT(h_lo[:, k, :], y2[:, k, :], h_hi[:, k, :].bitcast(F32), ALU.subtract).then_inc(s_y2v, 1)

            def add_ahead(u):
                m, h = divmod(u, 2)
                dve.wait_ge(s_unit, 2 * N_AOUT + u + 1)
                dve.wait_ge(s_x1r[m % 2], 16 * (m // 2 + 1))
                dve.wait_ge(s_y2v, m // 2 + 1)
                if counted((m + 1) // 2):
                    dve.wait_ge(s_y2l, (m + 1) // 2)
                TT(y2[:, m, halves(h)], ps[:, B_PROJ + h, :], (qn, kn)[m % 2][:, halves(h)],
                   ALU.add).then_inc(s_pre, 1)

            first = steps[0] + iteration(0, True, False, False, steps[0])
            per = iteration(1, True, True, False, first)
            with dve.Fori(2, PAIRS) as it:
                iteration(it, True, True, True, first + (it - 1) * per)
            iteration(PAIRS, False, True, True, first + (PAIRS - 1) * per)
            add_ahead(6)
            add_ahead(7)
            pt_low(PAIRS, CHUNK0[7])
            out_sum(PAIRS, 7)
            out_gate(PAIRS, 7)
            for h in range(2):
                dve.wait_ge(s_y2h, KT + h)
                TT(h_lo[:, KT - 1, halves(h)], y2[:, KT - 1, halves(h)],
                   h_hi[:, KT - 1, halves(h)].bitcast(F32), ALU.subtract).then_inc(s_y2v, 1)

            def add_out(m, h):
                dve.wait_ge(s_unit, 2 * (N_AOUT + m) + h + 1)
                dve.wait_ge(s_x1r[m % 2], 16 * (m // 2 + 1))
                dve.wait_ge(s_y2v, KT // 2 + 2)
                bank = (B_PROJ, B_PROJ + 1, B_OUT, B_MISC)[(2 * m + h) % 4]
                TT(y2[:, m, halves(h)], ps[:, bank, :], (qn, kn)[m % 2][:, halves(h)],
                   ALU.add).then_inc(s_or, 1)

            add_out(AHEAD, 0)
            add_out(AHEAD, 1)
            for u in range(2 * AHEAD):
                m, h = divmod(u, 2)
                dve.wait_ge(s_tail, u + 1)
                dve.wait_ge(s_pre, u + 1)
                TT(y2[:, m, halves(h)], ps[:, B_SCORE + u % 4, :], y2[:, m, halves(h)],
                   ALU.add).then_inc(s_fin, 1)
            for m in range(AHEAD + 1, KT):
                for h in range(2):
                    add_out(m, h)

        @block.gpsimd
        def _(pool):
            g = nc.gpsimd
            TT = g.tensor_tensor
            g.memset(ident[:, :], 0.0).then_inc(s_ident, 1)
            pool.wait_ge(s_ident, 1)
            g.affine_select(out=ident[:, :], in_=ident[:, :], compare_op=ALU.not_equal, fill=1.0, base=0,
                            pattern=[[-1, P]], channel_multiplier=1).then_inc(s_ident, 1)
            g.memset(acc, 0.0).then_inc(s_zero, 1)
            pool.wait_ge(s_zero, 1)
            pool.wait_ge(s_vconst, 1)
            pool.wait_ge(s_ident, 2)
            g.affine_select(out=mask_bf[:, 0:P], in_=mask_bf[:, 0:P], compare_op=ALU.is_ge, fill=MASKED,
                            base=0, pattern=[[-1, P]], channel_multiplier=1)
            g.tensor_copy(ident_bf[:, :], ident[:, :]).then_inc(s_ident, 1)

            def w_low(n, slot):
                pool.wait_ge(s_whi, n + 1)
                TT(w_lo[:, slot, :, :], w_raw[:, slot, :, :], w_hi[:, slot, :, :].bitcast(F32),
                   ALU.subtract).then_inc(s_wlo, 1)

            w_low(0, 0)
            for k in range(KT):
                pool.wait_ge(s_sqm, k + 1)
                if k:
                    pool.wait_ge(s_sqa, k)
                TT(acc[:, halves(0)], acc[:, halves(0)], sq2[:, halves(k % 2)], ALU.add).then_inc(s_sqa, 1)
                if k == 1:
                    w_low(1, 1)

            def conv_block(j, first):
                for t in range(4):
                    if not first or t:
                        w_low(4 * j + t + 1, (t + 1) % 2)
                    if t == 2:
                        for h in range(2):
                            pool.wait_ge(s_evac, 8 * j + 2 + h + 1)
                            pool.wait_ge(s_inv, 1)
                            us = ubuf[:, 2 + h * HALF:2 + (h + 1) * HALF]
                            TT(us, us, inv[:, halves(h)], ALU.mult).then_inc(s_u, 1)

            conv_block(0, True)
            with pool.Fori(1, KT) as j:
                conv_block(j, False)

            pool.wait_ge(s_ylo, 2 * KT)
            g.memset(acc, 0.0).then_inc(s_zero, 1)
            pool.wait_ge(s_zero, 2)
            with pool.Fori(0, 2) as i:
                for t in range(4):
                    w_low(N_COUT + 4 * i + t + 1, (t + 1) % 2)
                    for h in range(2):
                        u = 8 * i + 2 * t + h
                        pool.wait_ge(s_sqm, 2 * KT + u + 1)
                        pool.wait_ge(s_sqa, KT + u)
                        TT(acc[:, halves(h)], acc[:, halves(h)], sq2[:, halves(h)], ALU.add)\
                            .then_inc(s_sqa, 1)
            w_low(N_AIN, 1)

            def normalise(it, i, par):
                pair = it - 1
                w = 2 * P * (STEPS[i][1] + 1)
                col = 2 * (i % 2) + par
                pool.wait_ge(s_rd, 16 * pair + 2 * i + par + 1)
                p = (p_big if i % 2 == 0 else p_small)[:, par, 0:w]
                TT(p, p, rdenom[:, col:col + 1].broadcast_to([P, w]), ALU.mult).then_inc(s_pn, 1)

            def square_lo(it, u):
                src = (qn, kn)[u // 2][:, halves(u % 2)]
                pool.wait_ge(s_qsq, 4 * it + u + 1)
                if u == 0:
                    if counted(2 * it):
                        pool.wait_ge(s_vtr, 2 * it)
                else:
                    pool.wait_ge(s_ssq, 4 * it + u)
                TT(sq_raw[:, :], src, src, ALU.mult).then_inc(s_sqp, 1)
                pool.wait_ge(s_sqp, 4 * it + u + 1)
                TT(sq_lo[:, :], sq_raw[:, :], sq_hi[:, :].bitcast(F32), ALU.subtract)\
                    .then_inc(s_sql, 1)

            def stack_k_lo(pair, side):
                r = DH * side
                pool.wait_ge(s_khi, 2 * pair + side + 1)
                TT(k2[r:r + DH, side, :], kn[r:r + DH, :], k1[r:r + DH, side, :].bitcast(F32),
                   ALU.subtract).then_inc(s_stk, 1)
                pool.wait_ge(s_stk, 2 * pair + side + 1)

            def y2_low(k):
                pool.wait_ge(s_y2h, k + 1)
                TT(h_lo[:, k, :], y2[:, k, :], h_hi[:, k, :].bitcast(F32), ALU.subtract).then_inc(s_y2l, 1)

            def iteration(it, proj, att):
                for i in range(8):
                    if proj and i % 2 == 0:
                        w_low(N_AIN + 4 * it + i // 2 + 1, (N_AIN + i // 2 + 1) % 2)
                    if not proj and i in (4, 5, 7):
                        n = N_AOUT + 2 + (4, 5, 7).index(i)
                        w_low(n, n % 2)
                    if att:
                        normalise(it, i, 0)
                    if att and i == 1 and proj:
                        pool.wait_ge(s_pn, 16 * it - 13)
                        stack_k_lo(it - 1, 1)
                    if not proj and i == 0:
                        y2_low(1)
                    if not proj and i == 2:
                        pool.wait_ge(s_pn, 16 * it - 11)
                        stack_k_lo(it - 1, 1)
                    if proj and i == 7:
                        if att:
                            pool.wait_ge(s_pn, 16 * it - 1)
                        else:
                            pool.wait_ge(s_wlo, N_AIN + 4 * it + 5)
                        stack_k_lo(it, 0)
                    if att:
                        normalise(it, i, 1)
                    if proj and 1 <= i <= 4:
                        square_lo(it, i - 1)
                    if not proj and i == 0:
                        y2_low(3)
                    if not proj and i == 1:
                        y2_low(5)
                        w_low(N_AOUT + 1, (N_AOUT + 1) % 2)

            iteration(0, True, False)
            iteration(1, True, True)
            with pool.Fori(2, PAIRS) as it:
                iteration(it, True, True)
            iteration(PAIRS, False, True)
            for n in range(N_AOUT + AHEAD + 1, N_TILES):
                w_low(n, n % 2)


def kernel(**inputs):
    import numpy as np
    import concourse.bacc as bacc
    from concourse.bass_utils import run_bass_kernel_spmd

    nc = bacc.Bacc("TRN2", target_bir_lowering=False, num_devices=1)

    def tiles(w, blocks, order):
        w = w.reshape(KT, P, blocks, KT, P).transpose(3, 2, 1, 0, 4)[:, order]
        return w.reshape(KT * blocks, P, KT, P)

    def rows(v):
        return np.moveaxis(v.reshape(*v.shape[:-1], KT, P), -1, 0)

    w_a = inputs["attn_w_in"][0]
    laid_out = {
        "x": inputs["x"][0].T.reshape(KT, P, S).transpose(1, 0, 2),
        "w_cin": tiles(inputs["conv_w_in"][0], 4, CONV_COLUMNS),
        "w_cout": tiles(inputs["conv_w_out"][0], 1, [0]),
        "w_ain": tiles(w_a[:, :4 * D], 4, ATTN_COLUMNS),
        "w_forget": w_a[:, 4 * D:].reshape(KT, P, NH).transpose(1, 0, 2),
        "w_aout": tiles(inputs["attn_w_out"][0], 1, [0]),
        "conv_gain": rows(inputs["conv_norm_g"][0]),
        "conv_taps": rows(inputs["conv_w"][0]),
        "attn_gain": rows(inputs["attn_norm_g"][0]),
        "b_forget": inputs["attn_b_f"][0].reshape(NH, 1),
        "q_gain": inputs["attn_q_norm_g"][0].reshape(DH, 1),
        "k_gain": inputs["attn_k_norm_g"][0].reshape(DH, 1),
    }
    arrays, args = {}, []
    for name, a in laid_out.items():
        a = np.ascontiguousarray(a)
        arrays[f"in_{name}"] = a
        args.append(nc.dram_tensor(f"in_{name}", a.shape, mybir.dt.from_np(a.dtype), kind="ExternalInput").ap())
    args.append(nc.dram_tensor("out", (P, KT, S), F32, kind="ExternalOutput").ap())
    hybrid(nc, *args)
    result = run_bass_kernel_spmd(nc, [arrays], core_ids=[0])
    return result.results[0]["out"].transpose(2, 1, 0).reshape(1, S, D)
```
